# Optimizing a Trainium2 kernel written in Bass

```python
import math
import jax, jax.numpy as jnp
from jax import lax
import numpy as np

D_MODEL = 1024
BATCH = 1
SEQ = 1024
DEPTH = 2

D_SSD = 1024
SSD_HEAD_DIM = 64
SSD_HEADS = D_SSD // SSD_HEAD_DIM
SSD_GROUPS = 4
SSD_STATE = 128
D_CONV = 5
CONV_CH = D_SSD + 2 * SSD_GROUPS * SSD_STATE
CHUNK = 128
D_FNO = 512
FNO_GROUPS = 4
FNO_GROUP_DIM = D_FNO // FNO_GROUPS
N_MEM = 256
MEM_HEADS = 4
D_MEM = 512
MEM_HEAD_DIM = D_MEM // MEM_HEADS
N_BRANCH = 3
EPS = 1e-6
IN_SIZES = (D_SSD, CONV_CH, 2 * SSD_HEADS, D_FNO, D_FNO, D_MEM, D_MEM, N_BRANCH * D_MODEL)
D_IN = sum(IN_SIZES)

kernel_name = "hybrid_ssd_fourier_memxattn_encoder"

def _offsets(sizes):
    out, acc = [], 0
    for s in sizes[:-1]:
        acc += s
        out.append(acc)
    return out

def rmsnorm(x, g):
    xf = x.astype(jnp.float32)
    y = xf * lax.rsqrt(jnp.mean(xf * xf, axis=-1, keepdims=True) + EPS)
    return (y * g.astype(jnp.float32)).astype(x.dtype)

def gated_group_rmsnorm(y, z, g):
    b, L, d = y.shape
    t = (y * jax.nn.silu(z)).astype(jnp.float32).reshape(b, L, SSD_GROUPS, d // SSD_GROUPS)
    t = t * lax.rsqrt(jnp.mean(t * t, axis=-1, keepdims=True) + EPS)
    return (t.reshape(b, L, d) * g.astype(jnp.float32)).astype(y.dtype)

def centred_depthwise_conv(u, w, bias):
    C = u.shape[-1]
    out = lax.conv_general_dilated(
        u, w.reshape(D_CONV, 1, C).astype(u.dtype), window_strides=(1,),
        padding=[(D_CONV // 2, D_CONV // 2)],
        dimension_numbers=("NWC", "WIO", "NWC"), feature_group_count=C)
    return out + bias.astype(u.dtype)

def segsum(a):
    T = a.shape[-1]
    a_rep = jnp.broadcast_to(a[..., :, None], a.shape + (T,))
    a_rep = jnp.where(jnp.tril(jnp.ones((T, T), bool), -1), a_rep, 0.0)
    out = jnp.cumsum(a_rep, axis=-2)
    return jnp.where(jnp.tril(jnp.ones((T, T), bool)), out, -jnp.inf)

def ssd_chunked(xdt, dtA, Bm, Cm):
    b, L, H, P = xdt.shape
    G, N = Bm.shape[-2:]
    R = H // G
    c = L // CHUNK
    X = xdt.reshape(b, c, CHUNK, G, R, P)
    A = dtA.reshape(b, c, CHUNK, G, R).transpose(0, 3, 4, 1, 2)
    Bc = Bm.reshape(b, c, CHUNK, G, N)
    Cc = Cm.reshape(b, c, CHUNK, G, N)
    A_cs = jnp.cumsum(A, axis=-1)
    Lmat = jnp.exp(segsum(A))
    CB = jnp.einsum("bclgn,bcsgn->bgcls", Cc, Bc)
    y_diag = jnp.einsum("bgcls,bgrcls,bcsgrp->bclgrp", CB, Lmat, X)
    decay_states = jnp.exp(A_cs[..., -1:] - A_cs)
    states = jnp.einsum("bclgn,bgrcl,bclgrp->bcgrpn", Bc, decay_states, X)
    states = jnp.concatenate([jnp.zeros_like(states[:, :1]), states], axis=1)
    chunk_decay = jnp.exp(segsum(jnp.pad(A_cs[..., -1], ((0, 0), (0, 0), (0, 0), (1, 0)))))
    prev_states = jnp.einsum("bgrzc,bcgrpn->bzgrpn", chunk_decay, states)[:, :-1]
    y_off = jnp.einsum("bclgn,bcgrpn,bgrcl->bclgrp", Cc, prev_states, jnp.exp(A_cs))
    return (y_diag + y_off).reshape(b, L, H, P)

def hybrid_layer(x, mem, norm_g, w_in, conv_w, conv_b, dt_bias, a_log, d_skip, ssd_norm_g,
                 mem_norm_g, w_kv, p_ssd, p_fno, p_mem, w_out):
    b, L, D = x.shape
    f32 = jnp.float32
    h = rmsnorm(x, norm_g)
    proj = h @ w_in
    z_s, xbc, dt_raw, u_f, z_f, q, z_m, gates = jnp.split(proj, _offsets(IN_SIZES), axis=-1)

    xbc = jax.nn.silu(centred_depthwise_conv(xbc, conv_w, conv_b))
    xs, Bm, Cm = jnp.split(xbc, [D_SSD, D_SSD + SSD_GROUPS * SSD_STATE], axis=-1)
    xs = xs.astype(f32).reshape(b, L, SSD_HEADS, SSD_HEAD_DIM)
    Bm = Bm.astype(f32).reshape(b, L, SSD_GROUPS, SSD_STATE)
    Cm = Cm.astype(f32).reshape(b, L, SSD_GROUPS, SSD_STATE)
    dt = jax.nn.softplus(dt_raw.astype(f32).reshape(b, L, 2, SSD_HEADS) + dt_bias.astype(f32))
    dtA = dt * (-jnp.exp(a_log.astype(f32)))
    flip = lambda t: jnp.flip(t, axis=1)
    y_fwd = ssd_chunked(xs * dt[:, :, 0, :, None], dtA[:, :, 0], Bm, Cm)
    y_bwd = flip(ssd_chunked(flip(xs * dt[:, :, 1, :, None]), flip(dtA[:, :, 1]), flip(Bm), flip(Cm)))
    y_s = (y_fwd + y_bwd + d_skip.astype(f32)[:, None] * xs).reshape(b, L, D_SSD).astype(x.dtype)
    y_s = gated_group_rmsnorm(y_s, z_s, ssd_norm_g)

    uf = u_f.astype(f32).reshape(b, L, FNO_GROUPS, FNO_GROUP_DIM)
    y_f = jnp.real(jnp.fft.fft2(uf, axes=(1, 3), norm="ortho")).reshape(b, L, D_FNO).astype(x.dtype)
    y_f = y_f * jax.nn.silu(z_f)

    kv = rmsnorm(mem, mem_norm_g) @ w_kv
    k, v = jnp.split(kv.reshape(b, N_MEM, 2, MEM_HEADS, MEM_HEAD_DIM), 2, axis=2)
    k, v = k[:, :, 0], v[:, :, 0]
    qh = q.reshape(b, L, MEM_HEADS, MEM_HEAD_DIM)
    s = jnp.einsum("blhd,bmhd->bhlm", qh, k).astype(f32) * (MEM_HEAD_DIM ** -0.5)
    pr = jax.nn.softmax(s, axis=-1).astype(x.dtype)
    y_m = jnp.einsum("bhlm,bmhd->blhd", pr, v).reshape(b, L, D_MEM) * jax.nn.silu(z_m)

    g = jax.nn.sigmoid(gates.astype(f32)).astype(x.dtype).reshape(b, L, N_BRANCH, D)
    merged = g[:, :, 0] * (y_s @ p_ssd) + g[:, :, 1] * (y_f @ p_fno) + g[:, :, 2] * (y_m @ p_mem)
    return x + merged @ w_out

def setup_inputs(seed: int = 0) -> dict:
    key = jax.random.key(seed)
    ks = jax.random.split(key, 20)
    nrm = lambda k, shape, fan_in: jax.random.normal(k, shape, jnp.float32) * (fan_in ** -0.5)
    x = jax.random.normal(ks[0], (BATCH, SEQ, D_MODEL), jnp.float32)
    mem = jax.random.normal(ks[1], (BATCH, N_MEM, D_MODEL), jnp.float32)
    norm_g = 1.0 + 0.02 * jax.random.normal(ks[2], (DEPTH, D_MODEL), jnp.float32)
    w_in = nrm(ks[3], (DEPTH, D_MODEL, D_IN), D_MODEL)
    conv_w = nrm(ks[4], (DEPTH, D_CONV, CONV_CH), D_CONV)
    conv_b = 0.02 * jax.random.normal(ks[5], (DEPTH, CONV_CH), jnp.float32)
    dt0 = jnp.exp(jax.random.uniform(ks[6], (DEPTH, 2, SSD_HEADS), jnp.float32,
                                     math.log(1e-3), math.log(1e-1)))
    dt_bias = dt0 + jnp.log(-jnp.expm1(-dt0))
    a_log = jnp.log(jax.random.uniform(ks[7], (DEPTH, 2, SSD_HEADS), jnp.float32, 1.0, 16.0))
    d_skip = 1.0 + 0.1 * jax.random.normal(ks[8], (DEPTH, SSD_HEADS), jnp.float32)
    ssd_norm_g = 1.0 + 0.02 * jax.random.normal(ks[9], (DEPTH, D_SSD), jnp.float32)
    mem_norm_g = 1.0 + 0.02 * jax.random.normal(ks[10], (DEPTH, D_MODEL), jnp.float32)
    w_kv = nrm(ks[11], (DEPTH, D_MODEL, 2 * D_MEM), D_MODEL)
    p_ssd = nrm(ks[12], (DEPTH, D_SSD, D_MODEL), D_SSD)
    p_fno = nrm(ks[13], (DEPTH, D_FNO, D_MODEL), D_FNO)
    p_mem = nrm(ks[14], (DEPTH, D_MEM, D_MODEL), D_MEM)
    w_out = nrm(ks[15], (DEPTH, D_MODEL, D_MODEL), D_MODEL)
    final_g = 1.0 + 0.02 * jax.random.normal(ks[16], (D_MODEL,), jnp.float32)
    return {"x": x, "mem": mem, "norm_g": norm_g, "w_in": w_in, "conv_w": conv_w,
            "conv_b": conv_b, "dt_bias": dt_bias, "a_log": a_log, "d_skip": d_skip,
            "ssd_norm_g": ssd_norm_g, "mem_norm_g": mem_norm_g, "w_kv": w_kv,
            "p_ssd": p_ssd, "p_fno": p_fno, "p_mem": p_mem, "w_out": w_out,
            "final_g": final_g}

def reference(x, mem, norm_g, w_in, conv_w, conv_b, dt_bias, a_log, d_skip, ssd_norm_g,
              mem_norm_g, w_kv, p_ssd, p_fno, p_mem, w_out, final_g):
    for i in range(DEPTH):
        x = hybrid_layer(x, mem, norm_g[i], w_in[i], conv_w[i], conv_b[i], dt_bias[i], a_log[i],
                         d_skip[i], ssd_norm_g[i], mem_norm_g[i], w_kv[i], p_ssd[i], p_fno[i],
                         p_mem[i], w_out[i])
    return rmsnorm(x, final_g)


_drawn_inputs = setup_inputs


def setup_inputs(seed=0):
    import zlib

    import numpy as np

    out = dict(_drawn_inputs(seed))
    spreads = {}
    factors = {'ssd_norm_g': 4.065, 'mem_norm_g': 8.0, 'final_g': 2.866}
    for name, (base, spread) in spreads.items():
        noise = np.random.default_rng([zlib.crc32(name.encode()), seed]).standard_normal(out[name].shape)
        drawn = base * np.exp(spread * noise) if base else spread * noise
        out[name] = __import__('jax').numpy.asarray(drawn.astype(out[name].dtype))
    for name, factor in factors.items():
        out[name] = (out[name] * factor).astype(out[name].dtype)
    return out
```

```python
from contextlib import ExitStack

import concourse.bass as bass
from concourse import mybir

ALU = mybir.AluOpType
ACT = mybir.ActivationFunctionType
AX = mybir.AxisListType
F32 = mybir.dt.float32
F16 = mybir.dt.float16

P = 128
D = 1024
L = 1024
DEPTH = 2
KT = D // P
PT = L // P
HALF = 512
COLS = 256
G = 4
HG = 4
HD = 64
NH = G * HG
M = 256
EPS = 1e-6
WS = 32.0
SLABS = 6 * G + 20 + 4
TERMS = ((0, 0), (0, 1), (1, 0))
CW, CB, DTB, ALOG, DSK, NPAR = 0, 80, 96, 128, 160, 176
COSC, SINC, LE, GE, GT, LT, IDENT, ONES = range(8)
PHASES = (("head", 1), ("norm", 4), ("mem", 1), ("dt", 4), ("prep", 1), ("group", G), ("reload", 1), ("merge", 2), ("out", 1))


class At:

    def enter(self, phase, lay=0, it=0):
        self.phase, self.lay, self.it = phase, lay, it


class Line:

    def __init__(self, sem, name, plan, step=1, opened=0, like=None):
        self.sem, self.name, self.step, self.opened = sem, name, step, opened
        self.plan = None if plan is None else plan.get(like or name, {})
        self.seen = {}

    def tick(self, at, key=None):
        events = self.seen.setdefault(at.phase, [])
        assert key is None or key not in events, (self.name, key)
        events.append(key)
        return self.sem, self.step

    def _n(self, phase):
        return len(self.plan.get(phase, ()))

    def _count(self, phase, lay, it, pos):
        if self.plan is None:
            return 1
        if phase == "pre":
            return pos
        per_layer = sum(self._n(p) * times for p, times in PHASES)
        total = self._n("pre") + pos
        if phase == "post":
            return total + DEPTH * per_layer
        for p, times in PHASES:
            if p == phase:
                break
            total += self._n(p) * times
        if self._n(phase) and not (isinstance(it, int) and it == 0):
            total = it * self._n(phase) + total
        if per_layer and not (isinstance(lay, int) and lay == 0):
            total = lay * per_layer + total
        return total

    def count(self, at):
        return self._count(at.phase, at.lay, at.it, len(self.seen.get(at.phase, ())))

    def begin(self, at, phase=None, it=None):
        return self._count(phase or at.phase, at.lay, at.it if it is None else it, 0)

    def reached(self, count):
        return self.sem, (count + self.opened) * self.step

    def now(self, at):
        return self.reached(self.count(at))

    def after(self, at, key, phase=None, it=None):
        if self.plan is None:
            return self.sem, 1
        phase = phase or at.phase
        pos = self.plan[phase].index(key)
        lay = 0 if phase == "pre" else at.lay
        return self.reached(self._count(phase, lay, at.it if it is None else it, pos + 1))


def build(nc, io, plan):
    x_in, mem_in, slabs, wdt_in, par_in, norm_g, mem_g, ssd_g, final_g, consts_in, dft_in, altc_in, altr_in, out_hbm, xs_hbm, ys_hbm = io
    lines = []

    with ExitStack() as ctx:
        def sb(name, shape, dt=F32, stack=ctx):
            return stack.enter_context(nc.sbuf_tensor(name, shape, dt))

        def line(name, step=1, opened=0, like=None):
            made = Line(ctx.enter_context(nc.semaphore(name)), name, plan, step, opened, like)
            lines.append(made)
            return made

        hT = sb("hT", [P, 2, KT, L], F16)
        raw = sb("raw", [P, 2, KT * COLS])
        w16 = sb("w16", [P, 2, 2, KT, COLS], F16)
        cst = sb("cst", [P, 8, P])
        par = sb("par", [P, NPAR])
        dt_ = sb("dt_", [P, 2, PT, NH])
        ea = sb("ea", [P, 2, PT, NH])
        dd = sb("dd", [P, 2, PT, NH])
        tot = sb("tot", [P, 2, PT, NH])
        da = sb("da", [P, 2, PT, NH])
        ssdg = sb("ssdg", [P, D])
        gcw = sb("gcw", [P, 4, 5])
        gcb = sb("gcb", [P, 4])
        gdt = sb("gdt", [P, 2, PT, HG])
        gea = sb("gea", [P, 2, PT, HG])
        gdd = sb("gdd", [P, 2, PT, HG])
        gtot = sb("gtot", [P, 2, PT, HG])
        gda = sb("gda", [P, 2, PT, HG])
        gdk = sb("gdk", [P, HG])
        memT = sb("memT", [P, 2, KT, M], F16)
        rs = sb("rs", [P, 16])
        rr = sb("rr", [P, 16])

        head_mem = ExitStack()
        X = sb("X", [P, PT, D], F32, head_mem)
        grow = sb("grow", [P, 2, D], F32, head_mem)
        memX = sb("memX", [P, 2, D], F32, head_mem)
        hn = sb("hn", [P, 2, D], F32, head_mem)
        junk = sb("junk", [P, D], F32, head_mem)
        wdt_raw = sb("wdt_raw", [P, KT * 32], F32, head_mem)
        wdt = sb("wdt", [P, 2, KT, 32], F16, head_mem)
        sp_t = sb("sp_t", [P, 6, 2 * PT * NH], F32, head_mem)
        xout = sb("xout", [P, 2, D], F32, head_mem)
        head_mem.close()

        group_mem = ExitStack()
        pre = sb("pre", [P, 2, L + 4], F32, group_mem)
        cv = sb("cv", [P, 2, L], F32, group_mem)
        bct = sb("bct", [P, 2, L], F32, group_mem)
        xs_p = sb("xs_p", [P, PT, COLS], F32, group_mem)
        b_p = sb("b_p", [P, PT, P], F32, group_mem)
        zs = sb("zs", [P, PT, COLS], F32, group_mem)
        Y = sb("Y", [P, PT, COLS], F32, group_mem)
        bnd = sb("bnd", [P, 2, 2, HG, P], F32, group_mem)
        E = sb("E", [P, HG, P], F32, group_mem)
        cbm = sb("cbm", [P, 2, P], F32, group_mem)
        Mx = sb("Mx", [P, 2, HG, P], F32, group_mem)
        xw = sb("xw", [P, 2, 4, HG, HD], F32, group_mem)
        S = sb("S", [P, 2, HG, HD], F32, group_mem)
        yt = sb("yt", [P, 2, HG, HD], F32, group_mem)
        qT = sb("qT", [P, L], F32, group_mem)
        kT = sb("kT", [P, M], F32, group_mem)
        vM = sb("vM", [P, 2, P], F32, group_mem)
        zg = sb("zg", [P, L], F32, group_mem)
        th = sb("th", [P, HALF], F32, group_mem)
        pq16 = sb("pq16", [P, 2, 2, HALF], F16, group_mem)
        ny16 = sb("ny16", [1, 2, P], F16, group_mem)
        qs = sb("qs", [P, HALF], F32, group_mem)
        yo = sb("yo", [P, HALF], F32, group_mem)
        st16 = sb("st16", [P, 2, 2, HALF], F16, group_mem)
        dft = sb("dft", [P, 2, 2, 4, HALF], F16, group_mem)
        altc = sb("altc", [P, 2], F16, group_mem)
        altr = sb("altr", [1, HALF], F16, group_mem)
        att = sb("att", [P, 4, 4], F32, group_mem)
        group_mem.close()
        uT = zs[:, 0:4, :].rearrange("p a b -> p (a b)")
        uf = zs[:, 4:8, :].rearrange("p (e a) b -> p e (a b)", e=2)
        yf = uT
        probs = cv[:].rearrange("p b (r m) -> p (b r) m", m=M).rearrange("p (j n) m -> p j n m", n=2)
        pT = pre[:, :, 2:L + 2]

        merge_mem = ExitStack()
        yT = sb("yT", [P, 16, 2, L], F16, merge_mem)
        mT = sb("mT", [P, 2, KT, L], F16, merge_mem)
        acc = sb("acc", [P, 4, HALF], F32, merge_mem)
        tg = sb("tg", [P, 2, 4, HALF], F32, merge_mem)
        merge_mem.close()

        bank = [ctx.enter_context(nc.psum_tensor(f"bank{b}", [P, HALF], F32)) for b in range(8)]

        full = [line(f"full{b}") for b in range(8)]
        free = [line(f"free{b}", opened=1, like=f"full{b}") for b in range(8)]
        raw_in = [line(f"raw_in{p}", step=16) for p in range(2)]
        w_hi = [line(f"w_hi{p}") for p in range(2)]
        w_lo = [line(f"w_lo{p}", opened=1) for p in range(2)]
        taken = [Line(None, f"taken{p}", plan) for p in range(2)]
        lines.extend(taken)
        start_in = line("start_in", step=16)
        par_in_s = line("par_in_s", step=16)
        dft_in_s = line("dft_in_s", step=16)
        x_saved = line("x_saved", step=16)
        x_back = line("x_back", step=16)
        y_back = line("y_back", step=16)
        spill = [line(f"spill{r}", step=16, opened=1) for r in range(2)]
        out_done = [line(f"out_done{r}", step=16) for r in range(2)]
        chain = line("chain")
        act_s = line("act_s")
        dve_s = line("dve_s")
        hn_ready = line("hn_ready")
        split_hi = line("split_hi")
        split_lo = line("split_lo")
        conv_done = line("conv_done")
        th_ready = line("th_ready")
        th_used = line("th_used", opened=1)
        silu_done = line("silu_done")
        pool_init = line("pool_init")
        bnd_ready = line("bnd_ready")
        x_ready = line("x_ready", opened=1)
        e_ready = line("e_ready")
        m_ready = line("m_ready")
        s_ready = [line(f"s_ready{d}") for d in range(2)]
        o_in = line("o_in")
        o_hi = [line(f"o_hi{r}") for r in range(2)]
        o_lo = [line(f"o_lo{r}") for r in range(2)]
        tanhs = Line(None, "tanhs", plan)
        lines.append(tanhs)
        act_chain = line("act_chain")
        t_used = line("t_used", opened=8)
        m_in = line("m_in")
        m_hi = line("m_hi")
        m_lo = line("m_lo")
        x_done = line("x_done", opened=1)

        ident = cst[:, IDENT, :]
        GROUP_SLABS = ("XS", "BC", "KV", "UF", "QM", "Z")
        MERGE_SLABS = tuple(f"{n}{j}" for j in range(2) for n in ("G0", "PS", "G1", "G2", "PF"))
        OUT_SLABS = ("O0", "O1", "O2", "O3")
        block = ctx.enter_context(nc.Block())

        @block.sync
        def _(sp):
            at = At()
            at.enter("pre")
            for t, s in ((X[:], x_in.rearrange("(t p) d -> p t d", p=P)), (cst[:], consts_in)):
                sp.dma_start(t, s).then_inc(*start_in.tick(at))

            def load(slot, row):
                sp.wait_ge(*w_lo[slot].reached(raw_in[slot].count(at)))
                src = slabs[row] if isinstance(row, int) else slabs[bass.ds(row, 1)].rearrange("a p n -> (a p) n")
                sp.dma_start(raw[:, slot, :], src).then_inc(*raw_in[slot].tick(at))

            with sp.Fori(0, DEPTH) as lay:
                at.enter("head", lay)
                for s in (0, 1):
                    load(s, lay * SLABS + s)
                sp.wait_ge(*start_in.reached(2))
                sp.wait_ge(*x_done.reached(x_done.begin(at)))
                sp.dma_start(xs_hbm.rearrange("(t p) d -> p t d", p=P), X[:]).then_inc(*x_saved.tick(at))
                sp.dma_start(par[:], par_in[bass.ds(lay, 1)].rearrange("a p n -> (a p) n")).then_inc(*par_in_s.tick(at))
                sp.dma_start(wdt_raw[:], wdt_in[bass.ds(lay, 1)].rearrange("a p n -> (a p) n")).then_inc(*par_in_s.tick(at))
                sp.dma_start(memX[:], mem_in.rearrange("(t p) d -> p t d", p=P)).then_inc(*par_in_s.tick(at))
                for row, dst in ((norm_g, grow[:, 0, :]), (mem_g, grow[:, 1, :]), (ssd_g, ssdg[:])):
                    sp.dma_start(dst, row[bass.ds(lay, 1)].rearrange("a n -> (a n)").partition_broadcast(P))\
                        .then_inc(*par_in_s.tick(at))
                sp.dma_start(dft[:].rearrange("p a b c d -> p (a b c d)"), dft_in).then_inc(*dft_in_s.tick(at))
                sp.dma_start(altc[:], altc_in).then_inc(*dft_in_s.tick(at))
                sp.dma_start(altr[:], altr_in).then_inc(*dft_in_s.tick(at))
                with sp.Fori(0, G) as g:
                    at.enter("group", lay, g)

                    def send(r, key, block_row, half):
                        sp.wait_ge(*o_lo[r].after(at, key))
                        dst = ys_hbm[bass.ds(block_row, 1)].rearrange("a p (c l) -> (a p) c l", c=2)[:, :, half * HALF:(half + 1) * HALF]
                        sp.dma_start(dst, st16[:, r]).then_inc(*spill[r].tick(at, key))

                    for s in range(2, 8):
                        load(s % 2, lay * SLABS + g * 6 + s)
                    for half in range(2):
                        send(half, ("f", half), g + 8, half)
                    for half in range(2):
                        send(half, ("m", half), g + 12, half)
                    for n, (blk, half) in enumerate(((0, 0), (0, 1), (1, 0), (1, 1))):
                        send(n % 2, ("s", n), g * 2 + blk, half)
                at.enter("reload", lay)
                for r in range(2):
                    sp.wait_ge(*spill[r].reached(spill[r].begin(at)))
                for half in range(2):
                    sp.dma_start(yT[:, 8 * half:8 * half + 8].rearrange("p b c l -> p b (c l)"),
                                 ys_hbm[8 * half:8 * half + 8].rearrange("b p n -> p b n")).then_inc(*y_back.tick(at, half))
                with sp.Fori(0, 2) as jj:
                    at.enter("merge", lay, jj)
                    for s in range(10):
                        load(s % 2, lay * SLABS + jj * 10 + (26 + s))
                at.enter("out", lay)
                load(0, lay * SLABS + 46)
                sp.wait_ge(*full[3].after(at, ("PS1", 3), "merge", 1))
                sp.dma_start(X[:], xs_hbm.rearrange("(t p) d -> p t d", p=P)).then_inc(*x_back.tick(at))
                load(1, lay * SLABS + 47)
            at.enter("post")
            sp.wait_ge(*x_done.reached(x_done.begin(at)))
            sp.dma_start(grow[:, 0, :], final_g.partition_broadcast(P)).then_inc(*par_in_s.tick(at))
            for t in range(PT):
                sp.wait_ge(*hn_ready.after(at, ("f", t)))
                sp.dma_start(out_hbm[t * P:(t + 1) * P, :], xout[:, t % 2, :]).then_inc(*out_done[t % 2].tick(at, t))
            for r in range(2):
                sp.wait_ge(*out_done[r].now(at))

        @block.tensor
        def _(pe):
            at = At()
            at.enter("pre")
            pe.wait_ge(*start_in.reached(2))

            def use(b):
                pe.wait_ge(*free[b].reached(full[b].count(at)))

            def slab_ready(slot):
                taken[slot].tick(at)
                pe.wait_ge(*w_lo[slot].reached(taken[slot].count(at)))

            def products(out, lhs, rhs, kts, first=True, last=True):
                for k in kts:
                    for n, (a, b) in enumerate(TERMS):
                        mm = nc.tensor.matmul(out, lhs(a, k), rhs(b, k), start=first and k == kts[0] and n == 0,
                                              stop=last and k == kts[-1] and n == 2)
                return mm

            def channel_tile(key, b, slot, blk, half, data, kts=range(KT), off=0):
                use(b)
                return products(bank[b][:], lambda a, k: w16[:, slot, a, k, blk * P:(blk + 1) * P],
                                lambda c, k: data(c, k - off)[:, half * HALF:(half + 1) * HALF], kts)

            def channel_slab(name, slot, q, data=lambda c, k: hT[:, c, k, :]):
                if q == 0:
                    slab_ready(slot)
                channel_tile((name, q), q, slot, q // 2, q % 2, data).then_inc(*full[q].tick(at, (name, q)))

            def position_slab(name, slot, q, data):
                if q == 0:
                    slab_ready(slot)
                use(q)
                for j in range(2):
                    pt = 2 * q + j
                    mm = products(bank[q][:, j * COLS:(j + 1) * COLS],
                                  lambda a, k: data[:, a, k, pt * P:(pt + 1) * P],
                                  lambda b, k: w16[:, slot, b, k, :], range(KT))
                mm.then_inc(*full[q].tick(at, (name, q)))

            def turns(b, tiles, key):
                use(b)
                for n, t in enumerate(tiles):
                    mm = nc.tensor.transpose(bank[b][:, n * P:(n + 1) * P], t, ident)
                mm.then_inc(*full[b].tick(at, key))

            with pe.Fori(0, DEPTH) as lay:
                at.enter("head", lay)
                with pe.Fori(0, 4) as tt:
                    at.enter("norm", lay, tt)
                    for j in range(2):
                        pe.wait_ge(*hn_ready.after(at, ("h", j)))
                        for kk in range(2):
                            turns(2 * j + kk, [hn[:, j, (4 * kk + n) * P:(4 * kk + n + 1) * P] for n in range(4)], ("h", j, kk))
                at.enter("mem", lay)
                for j in range(2):
                    pe.wait_ge(*hn_ready.after(at, ("m", j)))
                    for kk in range(2):
                        turns(2 * j + kk, [hn[:, j, (4 * kk + n) * P:(4 * kk + n + 1) * P] for n in range(4)], ("m", j, kk))
                with pe.Fori(0, 4) as tt:
                    at.enter("dt", lay, tt)
                    pe.wait_ge(*split_lo.after(at, "h", "mem", 0))
                    pe.wait_ge(*dve_s.after(at, "wdt", "head", 0))
                    use(4)
                    for j in range(2):
                        mm = products(bank[4][:, j * 32:(j + 1) * 32],
                                      lambda a, k: hT[:, a, k, bass.ds(tt * (2 * P) + j * P, P)],
                                      lambda b, k: wdt[:, b, k, :], range(KT))
                    mm.then_inc(*full[4].tick(at, "dt"))
                at.enter("prep", lay)
                pe.wait_ge(*dve_s.after(at, "da"))
                use(4)
                f, bw = (da[:, d, :, :].rearrange("p c h -> p (c h)") for d in range(2))
                nc.tensor.matmul(bank[4][:, 0:P], cst[:, LE, :], f, start=True, stop=True)
                nc.tensor.matmul(bank[4][:, P:2 * P], cst[:, GE, :], bw, start=True, stop=True)
                nc.tensor.matmul(bank[4][:, 2 * P:3 * P], cst[:, GT, :], f, start=True, stop=True)
                nc.tensor.matmul(bank[4][:, 3 * P:4 * P], cst[:, LT, :], bw, start=True, stop=True)\
                    .then_inc(*full[4].tick(at, "cum"))
                use(5)
                nc.tensor.matmul(bank[5][:, 0:2 * P], cst[:, ONES, :], da[:].rearrange("p d c h -> p (d c h)"),
                                 start=True, stop=True).then_inc(*full[5].tick(at, "tot"))

                def step_in(i):
                    use(5)
                    c = slice(i * P, (i + 1) * P)
                    nc.tensor.matmul(bank[5][:, 0:P], bct[:, 0, c], bct[:, 1, c], start=True, stop=True)\
                        .then_inc(*full[5].tick(at, ("cb", i)))
                    pe.wait_ge(*bnd_ready.after(at, i))
                    use(6)
                    for d, mask in ((0, GT), (1, LT)):
                        mm = nc.tensor.matmul(bank[6][:], cst[:, mask, :], bnd[:, i % 2, d].rearrange("p h l -> p (h l)"),
                                              start=d == 0, stop=d == 1)
                    mm.then_inc(*full[6].tick(at, ("seg", i)))

                def step_out(i):
                    j = PT - 1 - i
                    ci, cj = slice(i * P, (i + 1) * P), slice(j * P, (j + 1) * P)
                    pe.wait_ge(*x_ready.after(at, i))
                    pe.wait_ge(*s_ready[0].after(at, i))
                    use(5)
                    nc.tensor.matmul(bank[5][:, 0:COLS], b_p[:, i, :], xw[:, i % 2, 2].rearrange("p h d -> p (h d)"),
                                     start=True, stop=True).then_inc(*full[5].tick(at, ("st", i)))
                    pe.wait_ge(*s_ready[1].after(at, i))
                    use(4)
                    nc.tensor.matmul(bank[4][:, 0:COLS], bct[:, 1, cj], S[:, 1].rearrange("p h d -> p (h d)"),
                                     start=True, stop=True)
                    nc.tensor.matmul(bank[4][:, COLS:HALF], b_p[:, j, :], xw[:, i % 2, 3].rearrange("p h d -> p (h d)"),
                                     start=True, stop=True).then_inc(*full[4].tick(at, ("bw", i)))
                    pe.wait_ge(*m_ready.after(at, i))
                    use(7)
                    nc.tensor.matmul(bank[7][:, COLS:HALF], bct[:, 1, ci], S[:, 0].rearrange("p h d -> p (h d)"),
                                     start=True, stop=True)
                    for h in range(HG):
                        for d in range(2):
                            mm = nc.tensor.matmul(bank[7][:, h * HD:(h + 1) * HD], Mx[:, d, h, :], xw[:, i % 2, d, h, :],
                                                  start=d == 0, stop=d == 1)
                    mm.then_inc(*full[7].tick(at, ("in", i)))

                def scores(j):
                    use(4)
                    if j == 0:
                        pe.wait_ge(*free[1].after(at, ("QM", 1)))
                    for n in range(2):
                        t = 2 * j + n
                        mm = nc.tensor.matmul(bank[4][:, n * M:(n + 1) * M], qT[:, t * P:(t + 1) * P], kT[:],
                                              start=True, stop=True)
                    mm.then_inc(*full[4].tick(at, ("sc", j)))

                def probs_turn(j):
                    pe.wait_ge(*dve_s.after(at, ("pr", j)))
                    turns(6, [probs[:, j, n, m * P:(m + 1) * P] for n in range(2) for m in range(2)], ("pt", j))

                with pe.Fori(0, G) as g:
                    at.enter("group", lay, g)
                    for q in range(4):
                        channel_slab("XS", 0, q)
                    for q in range(4):
                        channel_slab("BC", 1, q)
                    slab_ready(0)
                    use(0)
                    products(bank[0][:, 0:M], lambda a, k: w16[:, 0, a, k, 0:P], lambda b, k: memT[:, b, k, :], range(KT))\
                        .then_inc(*full[0].tick(at, "k"))
                    use(1)
                    for m in range(2):
                        mm = products(bank[1][:, m * P:(m + 1) * P], lambda a, k: memT[:, a, k, m * P:(m + 1) * P],
                                      lambda b, k: w16[:, 0, b, k, P:2 * P], range(KT))
                    mm.then_inc(*full[1].tick(at, "v"))
                    pe.wait_ge(*silu_done.after(at, "x1"))
                    for n in range(4):
                        turns(4 + n, [cv[:, blk, t * P:(t + 1) * P] for t in (2 * n, 2 * n + 1) for blk in range(2)], ("tx", n))
                    for q in range(4):
                        channel_slab("UF", 1, q)
                    pe.wait_ge(*silu_done.after(at, "B"))
                    for n in range(2):
                        turns(4 + n, [bct[:, 0, t * P:(t + 1) * P] for t in range(4 * n, 4 * n + 4)], ("tb", n))
                    pe.wait_ge(*dve_s.after(at, "fold"))
                    for n, (b, table) in enumerate(((6, COSC), (7, SINC))):
                        use(b)
                        for t in range(4):
                            mm = nc.tensor.matmul(bank[b][:, t * P:(t + 1) * P], uf[:, n, t * P:(t + 1) * P], cst[:, table, :],
                                                  start=True, stop=True)
                        mm.then_inc(*full[b].tick(at, ("dftc", n)))
                    use(4)
                    nc.tensor.matmul(bank[4][0:1, 0:P], uT[:, HALF:HALF + 1], cst[:, COSC, :], start=True, stop=True)\
                        .then_inc(*full[4].tick(at, "ny"))
                    channel_slab("QM", 0, 0)
                    pe.wait_ge(*dft_in_s.reached(dft_in_s.begin(at)))
                    pe.wait_ge(*split_lo.after(at, "ny"))
                    use(6)
                    products(bank[6][:], lambda a, t: pq16[:, 0, a, t * P:(t + 1) * P], lambda b, t: dft[:, 0, b, t, :],
                             range(4), last=False)
                    for a in range(2):
                        mm = nc.tensor.matmul(bank[6][:], ny16[0:1, a, :], altr[:], start=False, stop=a == 1)
                    mm.then_inc(*full[6].tick(at, "cos"))
                    use(7)
                    products(bank[7][:], lambda a, t: pq16[:, 1, a, t * P:(t + 1) * P], lambda b, t: dft[:, 1, b, t, :],
                             range(4)).then_inc(*full[7].tick(at, "sin"))
                    use(5)
                    for t in range(4):
                        for a in range(2):
                            nc.tensor.matmul(bank[5][:, 0:1], pq16[:, 0, a, t * P:(t + 1) * P], altc[:, 0:1],
                                             start=t == 0 and a == 0, stop=False)
                    for a in range(2):
                        mm = nc.tensor.matmul(bank[5][:, 0:1], ny16[0:1, a, :], altc[0:1, 0:1], start=False, stop=a == 1)
                    mm.then_inc(*full[5].tick(at, "mid"))
                    pe.wait_ge(*silu_done.after(at, "C"))
                    step_in(0)
                    pe.wait_ge(*free[5].after(at, ("tb", 1)))
                    for i in range(PT):
                        if i < 3:
                            channel_slab("QM", 0, i + 1)
                        elif i < 7:
                            scores(i - 3)
                            position_slab("Z", 1, i - 3, hT)
                        step_out(i)
                        if 3 <= i < 7:
                            probs_turn(i - 3)
                        if i < PT - 1:
                            step_in(i + 1)
                    pe.wait_ge(*free[6].after(at, ("pt", 3)))
                    for half in range(2):
                        use(6 + half)
                        for m in range(2):
                            mm = nc.tensor.matmul(bank[6 + half][:], vM[:, m, :], pT[:, m, half * HALF:(half + 1) * HALF],
                                                  start=m == 0, stop=m == 1)
                        mm.then_inc(*full[6 + half].tick(at, ("pv", half)))
                    pe.wait_ge(*dve_s.after(at, "yn"))
                    for n, (blk, half) in enumerate(((0, 0), (0, 1), (1, 0), (1, 1))):
                        turns(4 + n, [Y[:, t, blk * P:(blk + 1) * P] for t in range(4 * half, 4 * half + 4)], ("ty", n))

                with pe.Fori(0, 2) as jj:
                    at.enter("merge", lay, jj)
                    for j in range(2):
                        p0 = j % 2
                        for q in range(4):
                            channel_slab(f"G0{j}", p0, q)
                        pe.wait_ge(*y_back.reached(y_back.begin(at, "merge", 0)))
                        for q in range(4):
                            channel_slab(f"PS{j}", 1 - p0, q, lambda c, k: yT[:, k, c, :])
                        for q in range(4):
                            channel_slab(f"G1{j}", p0, q)
                        for q in range(4):
                            channel_slab(f"G2{j}", 1 - p0, q)
                        slab_ready(p0)
                        for name, kts in (("F", range(0, 4)), ("M", range(4, 8))):
                            for q in range(4):
                                channel_tile(None, q, p0, q // 2, q % 2, lambda c, k: yT[:, 8 + k, c, :], kts)\
                                    .then_inc(*full[q].tick(at, (f"P{name}{j}", q)))
                at.enter("out", lay)
                pe.wait_ge(*m_lo.reached(m_lo.begin(at)))
                for s, name in enumerate(OUT_SLABS):
                    for q in range(4):
                        position_slab(name, s % 2, q, mT)

        @block.scalar
        def _(act):
            at = At()
            at.enter("pre")

            def fill(slot):
                act.wait_ge(*raw_in[slot].reached(w_hi[slot].count(at) + 1))
                nc.scalar.activation(w16[:, slot, 0].rearrange("p k n -> p (k n)"), raw[:, slot, :], ACT.Copy, scale=WS)\
                    .then_inc(*w_hi[slot].tick(at))

            def tanh(dst, src, scale, key, waits=True):
                if waits:
                    act.wait_ge(*th_used.reached(th_ready.count(at)))
                nc.scalar.activation(dst, src, ACT.Tanh, scale=scale).then_inc(*th_ready.tick(at, key))

            def send_out(r, src, key):
                act.wait_ge(*spill[r].reached(o_hi[r].count(at)))
                nc.scalar.activation(st16[:, r, 0, :], src, ACT.Copy).then_inc(*o_hi[r].tick(at, key))

            def link(op):
                op.then_inc(*act_chain.tick(at))
                act.wait_ge(*act_chain.now(at))

            def squares(n, scrap, src, last):
                op = nc.scalar.activation(scrap, src, ACT.Square, accum_out=rs[:, n:n + 1])
                if last:
                    op.then_inc(*act_s.tick(at, "ss"))
                else:
                    link(op)

            def copy_bank(b, key, dst, src, scale, line=None, name=None):
                act.wait_ge(*full[b].after(at, key))
                nc.scalar.activation(dst, src, ACT.Copy, scale=scale).then_inc(*free[b].tick(at, key))

            act.wait_ge(*start_in.reached(2))
            with act.Fori(0, DEPTH) as lay:
                at.enter("head", lay)
                act.wait_ge(*x_done.reached(x_done.begin(at)))
                fill(0)
                act.wait_ge(*par_in_s.reached(par_in_s.begin(at, "norm")))
                for n in range(PT + 2):
                    squares(n, junk[:], X[:, n, :] if n < PT else memX[:, n - PT, :], n == PT + 1)
                act.wait_ge(*dve_s.after(at, "var"))
                nc.scalar.activation(rr[:, 0:PT + 2], rs[:, 0:PT + 2], ACT.Sqrt).then_inc(*act_s.tick(at, "rms"))
                with act.Fori(0, 4) as tt:
                    at.enter("norm", lay, tt)
                    for j in range(2):
                        for kk in range(2):
                            act.wait_ge(*full[2 * j + kk].after(at, ("h", j, kk)))
                            nc.scalar.activation(hT[:, 0, 4 * kk:4 * kk + 4, bass.ds(tt * (2 * P) + j * P, P)],
                                                 bank[2 * j + kk][:].rearrange("p (k l) -> p k l", k=4), ACT.Copy)\
                                .then_inc(*split_hi.tick(at, (j, kk)))
                at.enter("mem", lay)
                for j in range(2):
                    for kk in range(2):
                        act.wait_ge(*full[2 * j + kk].after(at, ("m", j, kk)))
                        nc.scalar.activation(memT[:, 0, 4 * kk:4 * kk + 4, j * P:(j + 1) * P],
                                             bank[2 * j + kk][:].rearrange("p (k l) -> p k l", k=4), ACT.Copy)\
                            .then_inc(*split_hi.tick(at, (j, kk)))
                at.enter("prep", lay)
                act.wait_ge(*dve_s.after(at, "abs"))
                nc.scalar.activation(sp_t[:, 1, :], sp_t[:, 1, :], ACT.Exp).then_inc(*act_s.tick(at, "exp"))
                nc.scalar.activation(par[:, ALOG:ALOG + 32], par[:, ALOG:ALOG + 32], ACT.Exp).then_inc(*act_s.tick(at, "A"))
                act.wait_ge(*dve_s.after(at, "1+exp"))
                nc.scalar.activation(sp_t[:, 3, :], sp_t[:, 2, :], ACT.Ln).then_inc(*act_s.tick(at, "ln"))
                act.wait_ge(*full[4].after(at, "cum"))
                nc.scalar.activation(ea[:].rearrange("p d c h -> p (d c h)"), bank[4][:, 0:2 * P], ACT.Exp)
                nc.scalar.activation(sp_t[:, 0, :], bank[4][:, 2 * P:4 * P], ACT.Exp).then_inc(*free[4].tick(at, "cum"))
                act.wait_ge(*full[5].after(at, "tot"))
                nc.scalar.activation(tot[:].rearrange("p d c h -> p (d c h)"), bank[5][:, 0:2 * P], ACT.Exp)\
                    .then_inc(*free[5].tick(at, "tot"))
                act.wait_ge(*x_saved.reached(x_saved.begin(at)))
                act.wait_ge(*dve_s.after(at, "prep"))

                with act.Fori(0, G) as g:
                    at.enter("group", lay, g)

                    def pre_copy(name, q):
                        act.wait_ge(*full[q].after(at, (name, q)))
                        dst = pre[:, q // 2, 2 + (q % 2) * HALF:2 + (q % 2 + 1) * HALF]
                        nc.scalar.activation(dst, bank[q][:], ACT.Copy, scale=0.5 / WS).then_inc(*free[q].tick(at, (name, q)))

                    def conv_tanh(key, src):
                        act.wait_ge(*conv_done.after(at, key))
                        tanh(th[:], src[:, 0:HALF], 1.0, (key, 0))
                        tanh(E[:].rearrange("p h l -> p (h l)"), src[:, HALF:L], 1.0, (key, 1), waits=False)

                    pre_copy("XS", 0)
                    fill(1)
                    pre_copy("XS", 1)
                    pre_copy("XS", 2)
                    conv_tanh("x0", cv[:, 0, :])
                    pre_copy("XS", 3)
                    conv_tanh("x1", cv[:, 1, :])
                    pre_copy("BC", 0)
                    fill(0)
                    pre_copy("BC", 1)
                    pre_copy("BC", 2)
                    conv_tanh("B", bct[:, 0, :])
                    pre_copy("BC", 3)
                    copy_bank(0, "k", kT[:], bank[0][:, 0:M], 1 / WS)
                    fill(1)
                    copy_bank(1, "v", vM[:].rearrange("p m d -> p (m d)"), bank[1][:, 0:2 * P], 1 / WS)
                    for n in range(4):
                        copy_bank(4 + n, ("tx", n), xs_p[:, 2 * n:2 * n + 2, :].rearrange("p t c -> p (t c)"), bank[4 + n][:], 1.0)
                    conv_tanh("C", bct[:, 1, :])
                    copy_bank(0, ("UF", 0), uT[:, 0:HALF], bank[0][:], 1 / WS)
                    fill(0)
                    copy_bank(1, ("UF", 1), uT[:, HALF:L], bank[1][:], 1 / WS)
                    for q in (2, 3):
                        act.wait_ge(*full[q].after(at, ("UF", q)))
                        tanh(th[:], bank[q][:], 0.5 / WS, ("UF", q))
                    for n in range(2):
                        copy_bank(4 + n, ("tb", n), b_p[:, 4 * n:4 * n + 4, :].rearrange("p t c -> p (t c)"), bank[4 + n][:], 1.0)
                    for n in range(2):
                        act.wait_ge(*full[6 + n].after(at, ("dftc", n)))
                        nc.scalar.activation(pq16[:, n, 0, :], bank[6 + n][:], ACT.Copy).then_inc(*split_hi.tick(at, ("dftc", n)))
                    act.wait_ge(*full[4].after(at, "ny"))
                    nc.scalar.activation(ny16[:, 0, :], bank[4][0:1, 0:P], ACT.Copy).then_inc(*split_hi.tick(at, "ny"))
                    copy_bank(0, ("QM", 0), qT[:, 0:HALF], bank[0][:], 1 / WS)
                    fill(1)
                    copy_bank(7, "sin", qs[:], bank[7][:], 1.0)
                    for half in range(2):
                        act.wait_ge(*o_in.after(at, ("f", half)))
                        send_out(half, yf[:, half * HALF:(half + 1) * HALF], ("f", half))
                    for i in range(PT):
                        act.wait_ge(*full[6].after(at, ("seg", i)))
                        if i >= 1:
                            act.wait_ge(*m_ready.after(at, i - 1))
                        nc.scalar.activation(E[:].rearrange("p h l -> p (h l)"), bank[6][:], ACT.Exp)\
                            .then_inc(*free[6].tick(at, ("seg", i)))
                        if i == 0:
                            copy_bank(1, ("QM", 1), qT[:, HALF:L], bank[1][:], 1 / WS)
                        elif i < 3:
                            act.wait_ge(*full[i + 1].after(at, ("QM", i + 1)))
                            tanh(th[:], bank[i + 1][:], 0.5 / WS, ("QM", i + 1))
                        elif i < 7:
                            j = i - 3
                            act.wait_ge(*dve_s.after(at, ("max", j)))
                            for n in range(2):
                                op = nc.scalar.activation(probs[:, j, n, :], bank[4][:, n * M:(n + 1) * M], ACT.Exp,
                                                          bias=att[:, 0, n:n + 1], scale=float(P) ** -0.5,
                                                          accum_out=att[:, 1, n:n + 1])
                            op.then_inc(*free[4].tick(at, ("sc", j)))
                            act.wait_ge(*full[j].after(at, ("Z", j)))
                            tanh(th[:], bank[j][:], 0.5 / WS, ("Z", j))
                            if j == 0:
                                fill(0)
                            copy_bank(6, ("pt", j), pT[:, :, 2 * j * P:(2 * j + 2) * P].rearrange("p m (n l) -> p n m l", n=2),
                                      bank[6][:].rearrange("p (n m l) -> p n m l", n=2, m=2), 1.0)
                    for t in range(PT):
                        act.wait_ge(*dve_s.after(at, ("yg", t // 2)))
                        squares(t, E[:].rearrange("p h l -> p (h l)")[:, 0:COLS], Y[:, t, :], t == PT - 1)
                    act.wait_ge(*dve_s.after(at, "var"))
                    nc.scalar.activation(rr[:, 0:PT], rs[:, 0:PT], ACT.Sqrt).then_inc(*act_s.tick(at, "rms"))
                    for half in range(2):
                        act.wait_ge(*o_in.after(at, ("m", half)))
                        send_out(half, yo[:], ("m", half))
                    for n in range(4):
                        act.wait_ge(*full[4 + n].after(at, ("ty", n)))
                        send_out(n % 2, bank[4 + n][:], ("s", n))

                with act.Fori(0, 2) as jj:
                    at.enter("merge", lay, jj)
                    for j in range(2):
                        for b in range(3):
                            name = f"G{b}{j}"
                            slot = (j + (0, 0, 1)[b]) % 2
                            for q in range(4):
                                act.wait_ge(*full[q].after(at, (name, q)))
                                act.wait_ge(*t_used.reached(tanhs.count(at) + (1 - 8)))
                                tanhs.tick(at)
                                op = nc.scalar.activation(tg[:, (3 * j + b) % 2, q, :], bank[q][:], ACT.Tanh, scale=0.5 / WS)
                                op.then_inc(*free[q].tick(at, (name, q)))
                                if q == 0:
                                    fill(1 - slot)
                            if b == 0:
                                act.wait_ge(*full[0].after(at, (f"PS{j}", 0)))
                                fill(slot)
                        act.wait_ge(*full[0].after(at, (f"PF{j}", 0)))
                        fill(1 - j)
                        for q in range(4):
                            kt = jj * 4 + (2 * j + q // 2)
                            act.wait_ge(*m_in.after(at, (j, q)))
                            nc.scalar.activation(mT[:, 0, bass.ds(kt, 1), (q % 2) * HALF:(q % 2 + 1) * HALF].rearrange("p k l -> p (k l)"),
                                                 acc[:, q, :], ACT.Copy, scale=0.5 / WS).then_inc(*m_hi.tick(at, (j, q)))
                at.enter("out", lay)
                for s in range(3):
                    act.wait_ge(*full[0].after(at, (OUT_SLABS[s], 0)))
                    fill(1 - s % 2)
            at.enter("post")
            act.wait_ge(*x_done.reached(x_done.begin(at)))
            for n in range(PT):
                squares(n, junk[:], X[:, n, :], n == PT - 1)
            act.wait_ge(*dve_s.after(at, "var"))
            nc.scalar.activation(rr[:, 0:PT], rs[:, 0:PT], ACT.Sqrt).then_inc(*act_s.tick(at, "rms"))

        @block.vector
        def _(dve):
            at = At()
            at.enter("pre")
            V = nc.vector
            for one in lines:
                if one.opened:
                    dve.sem_inc(one.sem, one.opened * one.step)

            def link(op):
                op.then_inc(*chain.tick(at))
                dve.wait_ge(*chain.now(at))

            def settle(one):
                dve.wait_ge(*one.now(at))

            def split_slab(slot):
                dve.wait_ge(*w_hi[slot].reached(w_lo[slot].count(at) + 1))
                V.scalar_tensor_tensor(w16[:, slot, 1].rearrange("p k n -> p (k n)"), raw[:, slot, :], WS,
                                       w16[:, slot, 0].rearrange("p k n -> p (k n)"), ALU.mult, ALU.subtract)\
                    .then_inc(*w_lo[slot].tick(at))

            def inverse_rms(n, width):
                dve.wait_ge(*act_s.after(at, "ss"))
                V.tensor_scalar(rs[:, 0:n], rs[:, 0:n], 1.0 / width, EPS, ALU.mult, ALU.add).then_inc(*dve_s.tick(at, "var"))
                dve.wait_ge(*act_s.after(at, "rms"))
                V.reciprocal(rr[:, 0:n], rr[:, 0:n]).then_inc(*dve_s.tick(at, "rr"))

            dve.wait_ge(*start_in.reached(2))
            with dve.Fori(0, DEPTH) as lay:
                at.enter("head", lay)
                dve.wait_ge(*par_in_s.reached(par_in_s.begin(at, "norm")))
                link(V.tensor_scalar(wdt[:, 0].rearrange("p k n -> p (k n)"), wdt_raw[:], WS, None, ALU.mult))
                V.scalar_tensor_tensor(wdt[:, 1].rearrange("p k n -> p (k n)"), wdt_raw[:], WS,
                                       wdt[:, 0].rearrange("p k n -> p (k n)"), ALU.mult, ALU.subtract)\
                    .then_inc(*dve_s.tick(at, "wdt"))
                link(V.tensor_scalar(par[:, CB:CB + 16], par[:, CB:CB + 16], 0.5, None, ALU.mult))
                split_slab(0)
                inverse_rms(PT + 2, D)

                def lo_part(dst, b, key, hi, freed):
                    dve.wait_ge(*split_hi.after(at, key))
                    V.tensor_tensor(dst, bank[b][:].rearrange("p (k l) -> p k l", k=4), hi, ALU.subtract)\
                        .then_inc(*free[b].tick(at, freed))

                with dve.Fori(0, 4) as tt:
                    at.enter("norm", lay, tt)
                    dve.wait_ge(*dve_s.after(at, "rr", "head", 0))
                    for j in range(2):
                        V.scalar_tensor_tensor(hn[:, j, :], X[:, bass.ds(2 * tt + j, 1), :].rearrange("p t d -> p (t d)"),
                                               rr[:, bass.ds(2 * tt + j, 1)], grow[:, 0, :], ALU.mult, ALU.mult)\
                            .then_inc(*hn_ready.tick(at, ("h", j)))
                    for j in range(2):
                        for kk in range(2):
                            at_l = bass.ds(tt * (2 * P) + j * P, P)
                            lo_part(hT[:, 1, 4 * kk:4 * kk + 4, at_l], 2 * j + kk, (j, kk),
                                    hT[:, 0, 4 * kk:4 * kk + 4, at_l], ("h", j, kk))
                at.enter("mem", lay)
                for j in range(2):
                    V.scalar_tensor_tensor(hn[:, j, :], memX[:, j, :], rr[:, PT + j:PT + j + 1], grow[:, 1, :],
                                           ALU.mult, ALU.mult).then_inc(*hn_ready.tick(at, ("m", j)))
                for j in range(2):
                    for kk in range(2):
                        lo_part(memT[:, 1, 4 * kk:4 * kk + 4, j * P:(j + 1) * P], 2 * j + kk, (j, kk),
                                memT[:, 0, 4 * kk:4 * kk + 4, j * P:(j + 1) * P], ("m", j, kk))
                dve.wait_ge(*free[3].after(at, ("m", 1, 1)))
                dve.sem_inc(*split_lo.tick(at, "h"))
                with dve.Fori(0, 4) as tt:
                    at.enter("dt", lay, tt)
                    dve.wait_ge(*full[4].after(at, "dt"))
                    for j in range(2):
                        op = V.scalar_tensor_tensor(dt_[:, :, bass.ds(2 * tt + j, 1), :].rearrange("p d c h -> p (d c) h"),
                                                    bank[4][:, j * 32:(j + 1) * 32].rearrange("p (d h) -> p d h", d=2), 1 / WS,
                                                    par[:, DTB:DTB + 32].rearrange("p (d h) -> p d h", d=2), ALU.mult, ALU.add)
                    op.then_inc(*free[4].tick(at, "dt"))
                at.enter("prep", lay)
                dve.wait_ge(*free[4].reached(free[4].begin(at)))
                v = dt_[:].rearrange("p d c h -> p (d c h)")
                V.scalar_tensor_tensor(sp_t[:, 1, :], v, -1.0, v, ALU.mult, ALU.min).then_inc(*dve_s.tick(at, "abs"))
                dve.wait_ge(*act_s.after(at, "A"))
                V.tensor_scalar(sp_t[:, 2, :], sp_t[:, 1, :], 1.0, None, ALU.add).then_inc(*dve_s.tick(at, "1+exp"))
                settle(dve_s)
                link(V.tensor_scalar(sp_t[:, 4, :], sp_t[:, 2, :], -1.0, None, ALU.add))
                link(V.tensor_scalar(sp_t[:, 5, :], sp_t[:, 4, :], 0.0, None, ALU.is_equal))
                link(V.tensor_tensor(sp_t[:, 4, :], sp_t[:, 4, :], sp_t[:, 5, :], ALU.add))
                link(V.reciprocal(sp_t[:, 4, :], sp_t[:, 4, :]))
                dve.wait_ge(*act_s.after(at, "ln"))
                link(V.tensor_tensor(sp_t[:, 3, :], sp_t[:, 3, :], sp_t[:, 5, :], ALU.add))
                link(V.tensor_tensor(sp_t[:, 3, :], sp_t[:, 3, :], sp_t[:, 4, :], ALU.mult))
                link(V.tensor_tensor(sp_t[:, 3, :], sp_t[:, 3, :], sp_t[:, 1, :], ALU.mult))
                link(V.scalar_tensor_tensor(v, v, 0.0, sp_t[:, 3, :], ALU.max, ALU.add))
                A = par[:, ALOG:ALOG + 32].rearrange("p (d h) -> p d h", d=2)
                for d in range(2):
                    op = V.scalar_tensor_tensor(da[:, d], dt_[:, d], -1.0, A[:, d].unsqueeze(1).to_broadcast([P, PT, NH]),
                                                ALU.mult, ALU.mult)
                op.then_inc(*dve_s.tick(at, "da"))
                dve.wait_ge(*free[4].after(at, "cum"))
                link(V.tensor_tensor(dd[:].rearrange("p d c h -> p (d c h)"), v, sp_t[:, 0, :], ALU.mult))
                dve.wait_ge(*free[5].after(at, "tot"))
                dve.wait_ge(*x_saved.reached(x_saved.begin(at)))
                for b in range(2):
                    V.memset(pre[:, b, 0:2], 0.0)
                    op = V.memset(pre[:, b, L + 2:L + 4], 0.0)
                op.then_inc(*dve_s.tick(at, "prep"))

                with dve.Fori(0, G) as g:
                    at.enter("group", lay, g)

                    def silu(dst, src, tanh_of, key, waits=True):
                        dve.wait_ge(*th_ready.after(at, key))
                        return V.scalar_tensor_tensor(dst, tanh_of, 1.0, src, ALU.add, ALU.mult)

                    def gate(q, key, dst):
                        silu(dst, bank[q][:], th[:], (key, q)).then_inc(*free[q].tick(at, (key, q)))
                        dve.wait_ge(*free[q].after(at, (key, q)))
                        dve.sem_inc(*th_used.tick(at, (key, q)))

                    def conv(key, blk, dst, n):
                        dve.wait_ge(*free[2 * blk + 1].after(at, ("XS" if n < 2 else "BC", 2 * blk + 1)))
                        link(V.tensor_scalar(dst, pre[:, blk, 0:L], gcw[:, n, 0:1], gcb[:, n:n + 1], ALU.mult, ALU.add))
                        for k in range(1, 5):
                            op = V.scalar_tensor_tensor(dst, pre[:, blk, k:k + L], gcw[:, n, k:k + 1], dst, ALU.mult, ALU.add)
                            if k < 4:
                                link(op)
                        op.then_inc(*conv_done.tick(at, key))

                    def conv_silu(key, dst):
                        settle(conv_done)
                        silu(dst[:, 0:HALF], dst[:, 0:HALF], th[:], (key, 0)).then_inc(*th_used.tick(at, (key, 0)))
                        silu(dst[:, HALF:L], dst[:, HALF:L], E[:].rearrange("p h l -> p (h l)"), (key, 1))\
                            .then_inc(*th_used.tick(at, (key, 1)))
                        dve.wait_ge(*th_used.now(at))
                        dve.sem_inc(*silu_done.tick(at, key))

                    V.tensor_copy(gcw[:].rearrange("p b k -> p (b k)"), par[:, bass.ds(g * 20 + CW, 20)])
                    V.tensor_copy(gcb[:], par[:, bass.ds(g * 4 + CB, 4)])
                    V.tensor_copy(gdk[:], par[:, bass.ds(g * HG + DSK, HG)])
                    for dst, src in ((gdt, dt_), (gea, ea), (gdd, dd), (gtot, tot), (gda, da)):
                        V.tensor_copy(dst[:].rearrange("p d c h -> p (d c) h"),
                                      src[:].rearrange("p d c h -> p (d c) h")[:, :, bass.ds(g * HG, HG)])
                    V.memset(S[:, 0].rearrange("p h d -> p (h d)"), 0.0).then_inc(*s_ready[0].tick(at, 0))
                    V.memset(S[:, 1].rearrange("p h d -> p (h d)"), 0.0).then_inc(*s_ready[1].tick(at, 0))
                    settle(s_ready[1])
                    dve.sem_inc(*dve_s.tick(at, "gc"))
                    split_slab(1)
                    conv("x0", 0, cv[:, 0, :], 0)
                    conv_silu("x0", cv[:, 0, :])
                    conv("x1", 1, cv[:, 1, :], 1)
                    conv_silu("x1", cv[:, 1, :])
                    split_slab(0)
                    conv("B", 0, bct[:, 0, :], 2)
                    conv_silu("B", bct[:, 0, :])
                    conv("C", 1, bct[:, 1, :], 3)
                    split_slab(1)
                    conv_silu("C", bct[:, 1, :])
                    split_slab(0)
                    dve.wait_ge(*free[1].after(at, ("UF", 1)))
                    V.tensor_tensor(uf[:, 0, 1:HALF], uT[:, 1:HALF], uT[:, L - 1:HALF:-1], ALU.add)
                    V.tensor_tensor(uf[:, 1, 1:HALF], uT[:, 1:HALF], uT[:, L - 1:HALF:-1], ALU.subtract)
                    V.tensor_copy(uf[:, 0, 0:1], uT[:, 0:1])
                    V.memset(uf[:, 1, 0:1], 0.0).then_inc(*dve_s.tick(at, "fold"))
                    for q in (2, 3):
                        gate(q, "UF", zg[:, (q - 2) * HALF:(q - 1) * HALF])
                    for n in range(2):
                        dve.wait_ge(*split_hi.after(at, ("dftc", n)))
                        V.tensor_tensor(pq16[:, n, 1, :], bank[6 + n][:], pq16[:, n, 0, :], ALU.subtract)\
                            .then_inc(*free[6 + n].tick(at, ("dftc", n)))
                    dve.wait_ge(*split_hi.after(at, "ny"))
                    V.tensor_tensor(ny16[:, 1, :], bank[4][0:1, 0:P], ny16[:, 0, :], ALU.subtract)\
                        .then_inc(*free[4].tick(at, "ny"))
                    dve.wait_ge(*free[4].after(at, "ny"))
                    dve.sem_inc(*split_lo.tick(at, "ny"))
                    split_slab(1)
                    dve.wait_ge(*full[6].after(at, "cos"))
                    dve.wait_ge(*free[7].after(at, "sin"))
                    V.tensor_tensor(yf[:, 0:HALF], bank[6][:], qs[:], ALU.subtract)
                    V.tensor_tensor(yf[:, L - 1:HALF:-1], bank[6][:, 1:HALF], qs[:, 1:HALF], ALU.add)\
                        .then_inc(*free[6].tick(at, "cos"))
                    dve.wait_ge(*full[5].after(at, "mid"))
                    V.tensor_copy(yf[:, HALF:HALF + 1], bank[5][:, 0:1]).then_inc(*free[5].tick(at, "mid"))
                    dve.wait_ge(*free[6].after(at, "cos"))
                    dve.wait_ge(*free[5].after(at, "mid"))
                    for half in range(2):
                        s = slice(half * HALF, (half + 1) * HALF)
                        V.scalar_tensor_tensor(yf[:, s], yf[:, s], float(L) ** -0.5 * 0.5 / WS, zg[:, s], ALU.mult, ALU.mult)\
                            .then_inc(*o_in.tick(at, ("f", half)))
                    for half in range(2):
                        dve.wait_ge(*o_hi[half].after(at, ("f", half)))
                        V.tensor_tensor(st16[:, half, 1, :], yf[:, half * HALF:(half + 1) * HALF], st16[:, half, 0, :], ALU.subtract)\
                            .then_inc(*o_lo[half].tick(at, ("f", half)))

                    def per_head(t, d, c):
                        return t[:, d, c, :].unsqueeze(2).to_broadcast([P, HG, HD])

                    for i in range(PT):
                        dve.wait_ge(*full[5].after(at, ("cb", i)))
                        V.tensor_tensor(cbm[:, 0, :], bank[5][:, 0:P], cst[:, LE, :], ALU.mult)
                        V.tensor_tensor(cbm[:, 1, :], bank[5][:, 0:P], cst[:, GE, :], ALU.mult)\
                            .then_inc(*free[5].tick(at, ("cb", i)))
                        dve.wait_ge(*free[5].after(at, ("cb", i)))
                        dve.wait_ge(*free[6].after(at, ("seg", i)))
                        for d in range(2):
                            op = V.tensor_tensor(Mx[:, d], E[:], cbm[:, d, :].unsqueeze(1).to_broadcast([P, HG, P]), ALU.mult)
                        op.then_inc(*m_ready.tick(at, i))
                        if 1 <= i < 3:
                            gate(i + 1, "QM", zg[:, (i - 1) * HALF:i * HALF])
                        elif 3 <= i < 7:
                            j = i - 3
                            dve.wait_ge(*full[4].after(at, ("sc", j)))
                            link(V.tensor_reduce(att[:, 0, 0:2], bank[4][:].rearrange("p (n m) -> p n m", n=2), AX.X, ALU.max))
                            V.tensor_scalar(att[:, 0, 0:2], att[:, 0, 0:2], -float(P) ** -0.5, None, ALU.mult)\
                                .then_inc(*dve_s.tick(at, ("max", j)))
                            dve.wait_ge(*free[4].after(at, ("sc", j)))
                            link(V.reciprocal(att[:, 2, 0:2], att[:, 1, 0:2]))
                            for n in range(2):
                                op = V.tensor_scalar(probs[:, j, n, :], probs[:, j, n, :], att[:, 2, n:n + 1], None, ALU.mult)
                            op.then_inc(*dve_s.tick(at, ("pr", j)))
                            gate(j, "Z", zs[:, 2 * j:2 * j + 2, :].rearrange("p t c -> p (t c)"))
                            if j == 0:
                                split_slab(0)
                        if i == 0:
                            dve.wait_ge(*pool_init.after(at, "Y"))
                        b = PT - 1 - i
                        yv = Y[:].rearrange("p t (h d) -> p t h d", h=HG)
                        dve.wait_ge(*full[4].after(at, ("bw", i)))
                        link(V.tensor_tensor(yt[:, 1], bank[4][:, 0:COLS].rearrange("p (h d) -> p h d", h=HG), per_head(gea, 1, b), ALU.mult))
                        V.tensor_tensor(yv[:, b], yv[:, b], yt[:, 1], ALU.add)
                        link(V.tensor_tensor(S[:, 1], S[:, 1], per_head(gtot, 1, b), ALU.mult))
                        V.tensor_tensor(S[:, 1], S[:, 1], bank[4][:, COLS:HALF].rearrange("p (h d) -> p h d", h=HG), ALU.add)\
                            .then_inc(*free[4].tick(at, ("bw", i)))
                        dve.wait_ge(*full[7].after(at, ("in", i)))
                        link(V.tensor_tensor(yt[:, 0], bank[7][:, COLS:HALF].rearrange("p (h d) -> p h d", h=HG), per_head(gea, 0, i), ALU.mult))
                        link(V.tensor_tensor(yt[:, 0], yt[:, 0], bank[7][:, 0:COLS].rearrange("p (h d) -> p h d", h=HG), ALU.add))
                        V.tensor_tensor(yv[:, i], yv[:, i], yt[:, 0], ALU.add).then_inc(*free[7].tick(at, ("in", i)))
                        dve.wait_ge(*full[5].after(at, ("st", i)))
                        link(V.tensor_tensor(S[:, 0], S[:, 0], per_head(gtot, 0, i), ALU.mult))
                        V.tensor_tensor(S[:, 0], S[:, 0], bank[5][:, 0:COLS].rearrange("p (h d) -> p h d", h=HG), ALU.add)\
                            .then_inc(*free[5].tick(at, ("st", i)))
                        dve.wait_ge(*free[5].after(at, ("st", i)))
                        if i < PT - 1:
                            dve.sem_inc(*s_ready[0].tick(at, i + 1))
                            dve.sem_inc(*s_ready[1].tick(at, i + 1))
                    for q in range(4):
                        V.scalar_tensor_tensor(Y[:, 2 * q:2 * q + 2, :], Y[:, 2 * q:2 * q + 2, :], 0.5 / WS,
                                               zs[:, 2 * q:2 * q + 2, :], ALU.mult, ALU.mult).then_inc(*dve_s.tick(at, ("yg", q)))
                    inverse_rms(PT, COLS)
                    settle(dve_s)
                    for t in range(PT):
                        op = V.scalar_tensor_tensor(Y[:, t, :], Y[:, t, :], rr[:, t:t + 1], ssdg[:, bass.ds(g * COLS, COLS)],
                                                    ALU.mult, ALU.mult)
                    op.then_inc(*dve_s.tick(at, "yn"))
                    for half in range(2):
                        dve.wait_ge(*full[6 + half].after(at, ("pv", half)))
                        V.scalar_tensor_tensor(yo[:], bank[6 + half][:], 0.5 / WS, zg[:, half * HALF:(half + 1) * HALF],
                                               ALU.mult, ALU.mult).then_inc(*free[6 + half].tick(at, ("pv", half)))
                        dve.wait_ge(*free[6 + half].after(at, ("pv", half)))
                        dve.sem_inc(*o_in.tick(at, ("m", half)))
                        dve.wait_ge(*o_hi[half].after(at, ("m", half)))
                        V.tensor_tensor(st16[:, half, 1, :], yo[:], st16[:, half, 0, :], ALU.subtract)\
                            .then_inc(*o_lo[half].tick(at, ("m", half)))
                        settle(o_lo[half])
                    for n in range(4):
                        dve.wait_ge(*o_hi[n % 2].after(at, ("s", n)))
                        V.tensor_tensor(st16[:, n % 2, 1, :], bank[4 + n][:], st16[:, n % 2, 0, :], ALU.subtract)\
                            .then_inc(*free[4 + n].tick(at, ("ty", n)))
                        dve.wait_ge(*free[4 + n].after(at, ("ty", n)))
                        dve.sem_inc(*o_lo[n % 2].tick(at, ("s", n)))

                with dve.Fori(0, 2) as jj:
                    at.enter("merge", lay, jj)
                    for j in range(2):
                        split_slab(1 - j)
                        for q in range(4):
                            dve.wait_ge(*free[q].after(at, (f"G0{j}", q)))
                            dve.wait_ge(*full[q].after(at, (f"PS{j}", q)))
                            V.scalar_tensor_tensor(acc[:, q, :], tg[:, (3 * j) % 2, q, :], 1.0, bank[q][:], ALU.add, ALU.mult)\
                                .then_inc(*free[q].tick(at, (f"PS{j}", q)))
                            dve.wait_ge(*free[q].after(at, (f"PS{j}", q)))
                            dve.sem_inc(*t_used.tick(at, (0, j, q)))
                            if q == 0:
                                split_slab(j)
                        split_slab(1 - j)
                        split_slab(j)
                        for b, name in ((1, "PF"), (2, "PM")):
                            for q in range(4):
                                dve.wait_ge(*free[q].after(at, (f"G{b}{j}", q)))
                                dve.wait_ge(*full[q].after(at, (f"{name}{j}", q)))
                                part = tg[:, (3 * j + b) % 2, q, :]
                                V.scalar_tensor_tensor(part, part, 1.0, bank[q][:], ALU.add, ALU.mult)\
                                    .then_inc(*free[q].tick(at, (f"{name}{j}", q)))
                                dve.wait_ge(*free[q].after(at, (f"{name}{j}", q)))
                                V.tensor_tensor(acc[:, q, :], acc[:, q, :], part, ALU.add).then_inc(*t_used.tick(at, (b, j, q)))
                                if b == 1 and q == 0:
                                    split_slab(1 - j)
                                if b == 2:
                                    settle(t_used)
                                    dve.sem_inc(*m_in.tick(at, (j, q)))
                        for q in range(4):
                            half = slice((q % 2) * HALF, (q % 2 + 1) * HALF)
                            kt = bass.ds(jj * 4 + (2 * j + q // 2), 1)
                            dve.wait_ge(*m_hi.after(at, (j, q)))
                            V.scalar_tensor_tensor(mT[:, 1, kt, half].rearrange("p k l -> p (k l)"), acc[:, q, :], 0.5 / WS,
                                                   mT[:, 0, kt, half].rearrange("p k l -> p (k l)"), ALU.mult, ALU.subtract)\
                                .then_inc(*m_lo.tick(at, (j, q)))
                at.enter("out", lay)
                dve.wait_ge(*x_back.reached(x_back.begin(at) + 1))
                for s, name in enumerate(OUT_SLABS):
                    for q in range(4):
                        dve.wait_ge(*full[q].after(at, (name, q)))
                        xv = X[:, 2 * q:2 * q + 2, s * COLS:(s + 1) * COLS]
                        V.scalar_tensor_tensor(xv, bank[q][:].rearrange("p (t c) -> p t c", t=2), 1 / WS, xv, ALU.mult, ALU.add)\
                            .then_inc(*free[q].tick(at, (name, q)))
                        if q == 0 and s < 3:
                            split_slab(1 - s % 2)
                dve.wait_ge(*free[3].after(at, ("O3", 3)))
                dve.sem_inc(*x_done.tick(at, "X"))
            at.enter("post")
            inverse_rms(PT, D)
            settle(dve_s)
            dve.wait_ge(*par_in_s.reached(par_in_s.begin(at) + 1))
            for t in range(PT):
                if t >= 2:
                    dve.wait_ge(*out_done[t % 2].after(at, t - 2))
                V.scalar_tensor_tensor(xout[:, t % 2, :], X[:, t, :], rr[:, t:t + 1], grow[:, 0, :], ALU.mult, ALU.mult)\
                    .then_inc(*hn_ready.tick(at, ("f", t)))

        @block.gpsimd
        def _(pool):
            at = At()
            at.enter("pre")
            Q = nc.gpsimd

            def heads(t, *at_):
                return t.unsqueeze(2).to_broadcast([P, HG, HD])

            with pool.Fori(0, DEPTH) as lay:
                with pool.Fori(0, G) as g:
                    at.enter("group", lay, g)

                    def step(i):
                        j = PT - 1 - i
                        if i >= 2:
                            pool.wait_ge(*full[7].after(at, ("in", i - 2)))
                        for d, mask in ((0, LE), (1, GE)):
                            op = Q.tensor_tensor(bnd[:, i % 2, d], cst[:, mask, :].unsqueeze(1).to_broadcast([P, HG, P]),
                                                 gda[:, d, i, :].unsqueeze(2).to_broadcast([P, HG, P]), ALU.mult)
                        op.then_inc(*bnd_ready.tick(at, i))
                        xi, xj = (xs_p[:, c, :].rearrange("p (h d) -> p h d", h=HG) for c in (i, j))
                        Q.tensor_tensor(xw[:, i % 2, 0], xi, heads(gdt[:, 0, i, :]), ALU.mult)
                        Q.tensor_tensor(xw[:, i % 2, 1], xi, heads(gdt[:, 1, i, :]), ALU.mult)
                        Q.tensor_tensor(xw[:, i % 2, 2], xi, heads(gdd[:, 0, i, :]), ALU.mult)
                        Q.tensor_tensor(xw[:, i % 2, 3], xj, heads(gdd[:, 1, j, :]), ALU.mult).then_inc(*x_ready.tick(at, i))

                    pool.wait_ge(*dve_s.after(at, "gc"))
                    pool.wait_ge(*free[7].after(at, ("tx", 3)))
                    for t in range(PT):
                        op = Q.tensor_tensor(Y[:, t, :].rearrange("p (h d) -> p h d", h=HG),
                                             xs_p[:, t, :].rearrange("p (h d) -> p h d", h=HG), heads(gdk[:]), ALU.mult)
                    op.then_inc(*pool_init.tick(at, "Y"))
                    step(0)
                    for i in range(1, PT):
                        step(i)

    for a, b in zip(full, free):
        for phase, _ in PHASES:
            assert sorted(map(str, a.seen.get(phase, []))) == sorted(map(str, b.seen.get(phase, []))), (a.name, phase)
    return {one.name: one.seen for one in lines}


def _slab(w):
    return w.reshape(KT, P, COLS).transpose(1, 0, 2).reshape(P, KT * COLS)


def _lay_out(inputs):
    import numpy as np

    w_in, w_kv = inputs["w_in"], inputs["w_kv"]
    z, xbc, dt, u, zf, q, zm, gt = 0, 1024, 3072, 3104, 3616, 4128, 4640, 5152
    slabs = []
    for i in range(DEPTH):
        w, kv = w_in[i], w_kv[i]
        for g in range(G):
            one = slice(g * P, (g + 1) * P)
            part = lambda m, off: m[:, off:][:, one]
            pair = lambda a, b: np.concatenate([a, b], axis=1)
            slabs += [w[:, xbc + g * COLS:xbc + (g + 1) * COLS],
                      pair(part(w, xbc + 1024), part(w, xbc + 1536)),
                      pair(part(kv, 0), part(kv, 512)),
                      pair(part(w, u), part(w, zf)),
                      pair(part(w, q), part(w, zm)),
                      w[:, z + g * COLS:z + (g + 1) * COLS]]
        for j in range(4):
            c = slice(j * COLS, (j + 1) * COLS)
            gates = [w[:, gt + b * D:gt + (b + 1) * D][:, c] for b in range(3)]
            fm = np.concatenate([inputs["p_fno"][i][:, c], inputs["p_mem"][i][:, c]], axis=0)
            slabs += [gates[0], inputs["p_ssd"][i][:, c], gates[1], gates[2], fm]
        slabs += [inputs["w_out"][i][:, s * COLS:(s + 1) * COLS] for s in range(4)]
    wdt = np.stack([w_in[i][:, dt:dt + 32].reshape(KT, P, 32).transpose(1, 0, 2).reshape(P, KT * 32) for i in range(DEPTH)])
    par = []
    for i in range(DEPTH):
        cw = inputs["conv_w"][i].T.reshape(16, P, 5)
        cb = inputs["conv_b"][i].reshape(16, P)
        order = [b for g in range(G) for b in (2 * g, 2 * g + 1, 8 + g, 12 + g)]
        rows = np.concatenate([inputs["dt_bias"][i].reshape(-1), inputs["a_log"][i].reshape(-1), inputs["d_skip"][i]])
        par.append(np.concatenate([cw[order].transpose(1, 0, 2).reshape(P, 80), cb[order].T,
                                   np.broadcast_to(rows, (P, 80))], axis=1))
    return np.stack([_slab(s) for s in slabs]), wdt, np.stack(par)


def _tables():
    import numpy as np

    p, f = np.arange(P)[:, None], np.arange(P)[None, :]
    turn = 2 * np.pi * p * f / P
    cst = np.stack([np.cos(turn) * P ** -0.5, np.sin(turn) * P ** -0.5, p <= f, p >= f, p > f, p < f, p == f,
                    np.ones((P, P))], axis=1).astype(np.float32)
    l, k = np.arange(HALF)[:, None], np.arange(HALF)[None, :]
    turn = 2 * np.pi * (l * k % L) / L
    dft = np.zeros((P, 2, 2, 4, HALF), np.float16)
    for n, t in enumerate((np.cos(turn), np.sin(turn))):
        t = t.reshape(4, P, HALF).transpose(1, 0, 2)
        hi = t.astype(np.float16)
        dft[:, n, 0], dft[:, n, 1] = hi, (t - hi).astype(np.float16)
    sign = (1 - 2 * (np.arange(HALF) % 2)).astype(np.float16)
    return cst, dft.reshape(P, -1), np.repeat(sign[:P, None], 2, axis=1), sign[None, :]


def kernel(**inputs):
    import numpy as np
    import concourse.bacc as bacc
    from concourse.bass_utils import run_bass_kernel_spmd

    inputs = {n: np.asarray(a) for n, a in inputs.items()}
    slabs, wdt, par = _lay_out(inputs)
    cst, dft, altc, altr = _tables()
    arrays = {"x": inputs["x"][0], "mem": inputs["mem"][0], "slabs": slabs, "wdt": wdt, "par": par,
              "norm_g": inputs["norm_g"], "mem_norm_g": inputs["mem_norm_g"], "ssd_norm_g": inputs["ssd_norm_g"],
              "final_g": inputs["final_g"], "cst": cst, "dft": dft, "altc": altc, "altr": altr}
    arrays = {f"in_{n}": np.ascontiguousarray(a) for n, a in arrays.items()}

    def program(plan):
        nc = bacc.Bacc("TRN2", target_bir_lowering=False, num_devices=1)
        io = [nc.dram_tensor(n, a.shape, mybir.dt.from_np(a.dtype), kind="ExternalInput").ap() for n, a in arrays.items()]
        io.append(nc.dram_tensor("out_0", (L, D), F32, kind="ExternalOutput").ap())
        io.append(nc.dram_tensor("x_scratch", (L, D), F32, kind="Internal").ap())
        io.append(nc.dram_tensor("y_scratch", (16, P, 2 * L), F16, kind="Internal").ap())
        return nc, build(nc, io, plan)

    _, plan = program(None)
    nc, _ = program(plan)
    r = run_bass_kernel_spmd(nc, [arrays], core_ids=[0])
    return r.results[0]["out_0"].reshape(1, L, D)
```

```python
from contextlib import ExitStack

import concourse.bass as bass
from concourse import mybir

ALU = mybir.AluOpType
ACT = mybir.ActivationFunctionType
AX = mybir.AxisListType
F32 = mybir.dt.float32
F16 = mybir.dt.float16

P = 128
D = 1024
L = 1024
DEPTH = 2
KT = D // P
PT = L // P
HALF = 512
COLS = 256
G = 4
HG = 4
HD = 64
NH = G * HG
M = 256
EPS = 1e-6
WS = 32.0
SLABS = 6 * G + 20 + 4
TERMS = ((0, 0), (0, 1), (1, 0))
CW, CB, DTB, ALOG, DSK, NPAR = 0, 80, 96, 128, 160, 176
COSC, SINC, LE, GE, GT, LT, IDENT, ONES = range(8)
PHASES = (("head", 1), ("norm", 1), ("first", 1), ("prep", 1), ("group", G), ("reload", 1), ("merge", 1), ("out", 1))


class At:

    def enter(self, phase, lay=0, it=0):
        self.phase, self.lay, self.it = phase, lay, it


class Line:

    def __init__(self, sem, name, plan, step=1, opened=0, like=None):
        self.sem, self.name, self.step, self.opened = sem, name, step, opened
        self.plan = None if plan is None else plan.get(like or name, {})
        self.seen = {}

    def tick(self, at, key=None):
        events = self.seen.setdefault(at.phase, [])
        assert key is None or key not in events, (self.name, key)
        events.append(key)
        return self.sem, self.step

    def _n(self, phase):
        return len(self.plan.get(phase, ()))

    def _count(self, phase, lay, it, pos):
        if self.plan is None:
            return 1
        if phase == "pre":
            return pos
        per_layer = sum(self._n(p) * times for p, times in PHASES)
        total = self._n("pre") + pos
        if phase == "post":
            return total + DEPTH * per_layer
        for p, times in PHASES:
            if p == phase:
                break
            total += self._n(p) * times
        if self._n(phase) and not (isinstance(it, int) and it == 0):
            total = it * self._n(phase) + total
        if per_layer and not (isinstance(lay, int) and lay == 0):
            total = lay * per_layer + total
        return total

    def count(self, at):
        return self._count(at.phase, at.lay, at.it, len(self.seen.get(at.phase, ())))

    def begin(self, at, phase=None, it=None):
        return self._count(phase or at.phase, at.lay, at.it if it is None else it, 0)

    def reached(self, count):
        return self.sem, (count + self.opened) * self.step

    def now(self, at):
        return self.reached(self.count(at))

    def after(self, at, key, phase=None, it=None):
        if self.plan is None:
            return self.sem, 1
        phase = phase or at.phase
        pos = self.plan[phase].index(key)
        lay = 0 if phase == "pre" else at.lay
        return self.reached(self._count(phase, lay, at.it if it is None else it, pos + 1))


def build(nc, io, plan):
    x_in, mem_in, slabs, wdt_in, par_in, norm_g, mem_g, ssd_g, consts_in, dft_in, altc_in, altr_in, out_hbm, xs_hbm, ys_hbm = io
    lines = []

    with ExitStack() as ctx:
        def sb(name, shape, dt=F32, stack=ctx):
            return stack.enter_context(nc.sbuf_tensor(name, shape, dt))

        def line(name, step=1, opened=0, like=None):
            made = Line(ctx.enter_context(nc.semaphore(name)), name, plan, step, opened, like)
            lines.append(made)
            return made

        hT = sb("hT", [P, 2, KT, L], F16)
        raw = sb("raw", [P, 2, KT * COLS])
        w16 = sb("w16", [P, 2, 2, KT, COLS], F16)
        cst = sb("cst", [P, 8, P])
        par = sb("par", [P, NPAR])
        dt_ = sb("dt_", [P, 2, PT, NH])
        ea = sb("ea", [P, 2, PT, NH])
        dd = sb("dd", [P, 2, PT, NH])
        tot = sb("tot", [P, 2, PT, NH])
        da = sb("da", [P, 2, PT, NH])
        ssdg = sb("ssdg", [P, D])
        gcw = sb("gcw", [P, 4, 5])
        gcb = sb("gcb", [P, 4])
        gea = sb("gea", [P, 2, PT, HG])
        gdd = sb("gdd", [P, 2, PT, HG])
        gtot = sb("gtot", [P, 2, PT, HG])
        mask16 = sb("mask16", [P, 4, P], F16)
        gdk = sb("gdk", [P, HG])
        memT = sb("memT", [P, 2, KT, M], F16)
        rs = sb("rs", [P, 16])
        rr = sb("rr", [P, 16])

        head_mem = ExitStack()
        X = sb("X", [P, PT, D], F32, head_mem)
        junk = sb("junk", [P, D], F32, head_mem)
        grow = sb("grow", [P, 2, D], F32, head_mem)
        hn = sb("hn", [P, PT + 2, D], F32, head_mem)
        memX = sb("memX", [P, 2, D], F32, head_mem)
        wdt_raw = sb("wdt_raw", [P, KT * 32], F32, head_mem)
        wdt = sb("wdt", [P, 2, KT, 32], F16, head_mem)
        sp_t = sb("sp_t", [P, 6, 2 * PT * NH], F32, head_mem)
        head_mem.close()

        group_mem = ExitStack()
        pre = sb("pre", [P, 2, L + 4], F32, group_mem)
        cv = sb("cv", [P, 2, L], F32, group_mem)
        bct = sb("bct", [P, 2, L], F32, group_mem)
        xs_p = sb("xs_p", [P, PT, COLS], F32, group_mem)
        b_p = sb("b_p", [P, PT, P], F32, group_mem)
        zs = sb("zs", [P, PT, COLS], F32, group_mem)
        Y = sb("Y", [P, PT, COLS], F32, group_mem)
        bnd = sb("bnd", [P, 2, 2, 2, HG, P], F16, group_mem)
        with ExitStack() as shared:
            E = sb("E", [P, HG, P], F32, shared)
        e16 = sb("e16", [P, 2, HALF], F16, group_mem)
        cbm = sb("cbm", [P, 2, P], F32, group_mem)
        W = sb("W", [P, 2, HG, P], F32, group_mem)
        Mx = sb("Mx", [P, HG, P], F32, group_mem)
        xw = sb("xw", [P, 2, 2, HG, HD], F32, group_mem)
        S = sb("S", [P, 2, HG, HD], F32, group_mem)
        yt = sb("yt", [P, 2, HG, HD], F32, group_mem)
        qT = sb("qT", [P, L], F32, group_mem)
        kT = sb("kT", [P, M], F32, group_mem)
        vM = sb("vM", [P, 2, P], F32, group_mem)
        zg = sb("zg", [P, L], F32, group_mem)
        th = sb("th", [P, HALF], F32, group_mem)
        pq16 = sb("pq16", [P, 2, 2, HALF], F16, group_mem)
        ny16 = sb("ny16", [1, 2, P], F16, group_mem)
        qs = sb("qs", [P, HALF], F32, group_mem)
        st16 = sb("st16", [P, 3, 2, HALF], F16, group_mem)
        dft = sb("dft", [P, 2, 2, 4, COLS], F16, group_mem)
        eo = sb("eo", [P, 2, HALF + 1], F32, group_mem)
        altc = sb("altc", [P, 2], F16, group_mem)
        altr = sb("altr", [1, COLS], F16, group_mem)
        gdt = sb("gdt", [P, 2, PT, HG], F32, group_mem)
        gda = sb("gda", [P, 2, 2, PT, HG], F16, group_mem)
        att = sb("att", [P, 4, 4], F32, group_mem)
        group_mem.close()
        uT = zs[:, 0:4, :].rearrange("p a b -> p (a b)")
        uf = zs[:, 4:8, :].rearrange("p (e a) b -> p e (a b)", e=2)
        yf = uT
        probs = cv[:].rearrange("p b (r m) -> p (b r) m", m=M).rearrange("p (j n) m -> p j n m", n=2)
        place = [st16[:, 0], st16[:, 1], st16[:, 2], e16[:]]
        pT = pre[:, :, 2:L + 2]

        merge_mem = ExitStack()
        yT = sb("yT", [P, 16, 2, L], F16, merge_mem)
        mT = sb("mT", [P, 2, KT, L], F16, merge_mem)
        acc = sb("acc", [P, 4, HALF], F32, merge_mem)
        tg = sb("tg", [P, 2, 4, HALF], F32, merge_mem)
        merge_mem.close()

        bank = [ctx.enter_context(nc.psum_tensor(f"bank{b}", [P, HALF], F32)) for b in range(8)]

        full = [line(f"full{b}") for b in range(8)]
        free = [line(f"free{b}", opened=1, like=f"full{b}") for b in range(8)]
        raw_in = [line(f"raw_in{p}", step=16) for p in range(2)]
        w_hi = [line(f"w_hi{p}") for p in range(2)]
        w_lo = [line(f"w_lo{p}", opened=1) for p in range(2)]
        taken = [Line(None, f"taken{p}", plan) for p in range(2)]
        lines.extend(taken)
        start_in = line("start_in", step=16)
        x_in_s = [line(f"x_in{half}", step=16) for half in range(2)]
        par_in_s = line("par_in_s", step=16)
        mem_in_s = line("mem_in_s", step=16)
        dft_in_s = line("dft_in_s", step=16)
        x_saved = line("x_saved", step=16)
        x_back = line("x_back", step=16)
        y_back = [line(f"y_back{half}", step=16) for half in range(2)]
        spill = [line(f"spill{r}", step=16, opened=1) for r in range(4)]
        out_done = line("out_done", step=16)
        gain_in = line("gain_in", step=16)
        chain = line("chain")
        act_s = line("act_s")
        dve_s = line("dve_s")
        hn_ready = line("hn_ready")
        split_hi = line("split_hi")
        split_lo = line("split_lo")
        conv_done = line("conv_done")
        th_ready = line("th_ready")
        th_used = line("th_used", opened=1)
        silu_done = line("silu_done")
        pool_init = line("pool_init")
        bnd_ready = line("bnd_ready")
        x_ready = line("x_ready", opened=1)
        e_ready = line("e_ready")
        w_ready = line("w_ready")
        pool_chain = line("pool_chain")
        m_ready = line("m_ready")
        s_ready = [line(f"s_ready{d}") for d in range(2)]
        o_in = line("o_in")
        o_hi = [line(f"o_hi{r}") for r in range(4)]
        o_lo = [line(f"o_lo{r}") for r in range(4)]
        tanhs = Line(None, "tanhs", plan)
        lines.append(tanhs)
        act_chain = line("act_chain")
        t_used = line("t_used", opened=8)
        m_in = line("m_in")
        m_hi = line("m_hi")
        m_lo = line("m_lo")
        x_done = line("x_done", opened=1)

        ident = cst[:, IDENT, :]
        GROUP_SLABS = ("XS", "BC", "KV", "UF", "QM", "Z")
        MERGE_SLABS = tuple(f"{n}{j}" for j in range(4) for n in ("G0", "G1", "PS", "G2", "PF"))
        OUT_SLABS = ("O0", "O1", "O2", "O3")
        block = ctx.enter_context(nc.Block())

        @block.sync
        def _(sp):
            at = At()
            at.enter("pre")
            for half in range(2):
                sp.dma_start(X[:, 4 * half:4 * half + 4], x_in.rearrange("(t p) d -> p t d", p=P)[:, 4 * half:4 * half + 4])\
                    .then_inc(*x_in_s[half].tick(at))
            sp.dma_start(cst[:], consts_in).then_inc(*start_in.tick(at))
            sp.dma_start(grow[:, 0, :], norm_g[0:1].rearrange("a n -> (a n)").partition_broadcast(P)).then_inc(*gain_in.tick(at))

            def load(slot, row):
                sp.wait_ge(*w_lo[slot].reached(raw_in[slot].count(at)))
                src = slabs[row] if isinstance(row, int) else slabs[bass.ds(row, 1)].rearrange("a p n -> (a p) n")
                sp.dma_start(raw[:, slot, :], src).then_inc(*raw_in[slot].tick(at))

            with sp.Fori(0, DEPTH) as lay:
                at.enter("head", lay)
                load(0, lay * SLABS)
                sp.wait_ge(*x_done.reached(x_done.begin(at)))
                sp.dma_start(par[:], par_in[bass.ds(lay, 1)].rearrange("a p n -> (a p) n")).then_inc(*par_in_s.tick(at))
                sp.dma_start(wdt_raw[:], wdt_in[bass.ds(lay, 1)].rearrange("a p n -> (a p) n")).then_inc(*par_in_s.tick(at))
                for row, dst in ((mem_g, grow[:, 1, :]), (ssd_g, ssdg[:])):
                    sp.dma_start(dst, row[bass.ds(lay, 1)].rearrange("a n -> (a n)").partition_broadcast(P))\
                        .then_inc(*mem_in_s.tick(at))
                sp.dma_start(memX[:], mem_in.rearrange("(t p) d -> p t d", p=P)).then_inc(*mem_in_s.tick(at))
                load(1, lay * SLABS + 1)
                load(0, lay * SLABS + 2)
                for half in range(2):
                    sp.wait_ge(*x_in_s[half].reached(1))
                sp.dma_start(xs_hbm.rearrange("(t p) d -> p t d", p=P), X[:]).then_inc(*x_saved.tick(at))
                sp.wait_ge(*dve_s.after(at, "prep", "prep", 0))
                sp.dma_start(dft[:].rearrange("p a b c d -> p (a b c d)"), dft_in).then_inc(*dft_in_s.tick(at))
                sp.dma_start(altc[:], altc_in).then_inc(*dft_in_s.tick(at))
                sp.dma_start(altr[:], altr_in).then_inc(*dft_in_s.tick(at))
                with sp.Fori(0, G) as g:
                    at.enter("group", lay, g)

                    def send(r, key, block_row, half):
                        sp.wait_ge(*o_lo[r].after(at, key))
                        dst = ys_hbm[bass.ds(block_row, 1)].rearrange("a p (c l) -> (a p) c l", c=2)[:, :, half * HALF:(half + 1) * HALF]
                        sp.dma_start(dst, place[r]).then_inc(*spill[r].tick(at, key))

                    for s in range(3, 8):
                        load(s % 2, lay * SLABS + g * 6 + s)
                    for half in range(2):
                        send(half, ("f", half), g + 8, half)
                    load(0, lay * SLABS + g * 6 + 8)
                    for half in range(2):
                        send(half, ("m", half), g + 12, half)
                    for n, (blk, half) in enumerate(((0, 0), (0, 1), (1, 0), (1, 1))):
                        send((2, 3, 0, 1)[n], ("s", n), g * 2 + blk, half)
                at.enter("reload", lay)
                for r in range(4):
                    sp.wait_ge(*spill[r].reached(spill[r].begin(at)))
                sp.wait_ge(*act_s.after(at, ("g0", 3), "merge", 0))
                for half in range(2):
                    sp.dma_start(yT[:, 8 * half:8 * half + 8].rearrange("p b c l -> p b (c l)"),
                                 ys_hbm[8 * half:8 * half + 8].rearrange("b p n -> p b n")).then_inc(*y_back[half].tick(at, half))
                at.enter("merge", lay)
                for n in range(1, 20):
                    load(n % 2, lay * SLABS + (26 + n))
                at.enter("out", lay)
                load(0, lay * SLABS + 46)
                sp.wait_ge(*full[3].after(at, ("PS3", 3), "merge", 0))
                sp.dma_start(X[:], xs_hbm.rearrange("(t p) d -> p t d", p=P)).then_inc(*x_back.tick(at))
                load(1, lay * SLABS + 47)
                sp.wait_ge(*full[3].after(at, ("PM3", 3), "merge", 0))
                sp.dma_start(grow[:, 0, :], norm_g[bass.ds(lay + 1, 1)].rearrange("a n -> (a n)").partition_broadcast(P))\
                    .then_inc(*gain_in.tick(at))
            at.enter("post")
            for t in range(PT):
                sp.wait_ge(*(hn_ready.reached(hn_ready.begin(at)) if t < 4 else hn_ready.after(at, ("h", t))))
                sp.dma_start(out_hbm[t * P:(t + 1) * P, :], hn[:, t, :]).then_inc(*out_done.tick(at, t))
            sp.wait_ge(*out_done.now(at))

        @block.tensor
        def _(pe):
            at = At()
            at.enter("pre")
            pe.wait_ge(*start_in.reached(1))

            def use(b):
                pe.wait_ge(*free[b].reached(full[b].count(at)))

            def slab_ready(slot):
                taken[slot].tick(at)
                pe.wait_ge(*w_lo[slot].reached(taken[slot].count(at)))

            def products(out, lhs, rhs, kts, first=True, last=True):
                for k in kts:
                    for n, (a, b) in enumerate(TERMS):
                        mm = nc.tensor.matmul(out, lhs(a, k), rhs(b, k), start=first and k == kts[0] and n == 0,
                                              stop=last and k == kts[-1] and n == 2)
                return mm

            def channel_tile(b, slot, blk, half, data, kts=range(KT), **ends):
                return products(bank[b][:], lambda a, k: w16[:, slot, a, k, blk * P:(blk + 1) * P],
                                lambda c, k: data(c, k)[:, half * HALF:(half + 1) * HALF], kts, **ends)

            def channel_slab(name, slot, q, data=lambda c, k: hT[:, c, k, :], parts=(0, 1)):
                if 0 in parts:
                    if q == 0:
                        slab_ready(slot)
                    use(q)
                mm = channel_tile(q, slot, q // 2, q % 2, data, range(6 * parts[0], (6, KT)[parts[-1]]),
                                  first=0 in parts, last=1 in parts)
                if 1 in parts:
                    mm.then_inc(*full[q].tick(at, (name, q)))

            def position_slab(name, slot, q, data, parts=(0, 1)):
                if 0 in parts:
                    if q == 0:
                        slab_ready(slot)
                    use(q)
                for j in parts:
                    pt = 2 * q + j
                    mm = products(bank[q][:, j * COLS:(j + 1) * COLS],
                                  lambda a, k: data[:, a, k, pt * P:(pt + 1) * P],
                                  lambda b, k: w16[:, slot, b, k, :], range(KT))
                if 1 in parts:
                    mm.then_inc(*full[q].tick(at, (name, q)))

            def turns(b, tiles, key):
                use(b)
                for n, t in enumerate(tiles):
                    mm = nc.tensor.transpose(bank[b][:, n * P:(n + 1) * P], t, ident)
                mm.then_inc(*full[b].tick(at, key))

            with pe.Fori(0, DEPTH) as lay:
                at.enter("head", lay)
                at.enter("norm", lay)
                for t in range(PT):
                    pe.wait_ge(*(hn_ready.reached(hn_ready.begin(at, "head") + (t - 3)) if t < 4 else hn_ready.after(at, ("h", t))))
                    for kk in range(2):
                        turns(2 * (t % 4) + kk, [hn[:, t, (4 * kk + n) * P:(4 * kk + n + 1) * P] for n in range(4)], ("h", t, kk))
                at.enter("first", lay)
                pe.wait_ge(*split_lo.after(at, "half h", "norm", 0))
                for q in (0, 2):
                    channel_slab("XS", 0, q)
                pe.wait_ge(*split_lo.after(at, "h"))
                pe.wait_ge(*dve_s.after(at, "wdt"))
                use(4)
                for t in range(PT):
                    mm = products(bank[4][:, t * 32:(t + 1) * 32], lambda a, k: hT[:, a, k, t * P:(t + 1) * P],
                                  lambda b, k: wdt[:, b, k, :], range(KT))
                mm.then_inc(*full[4].tick(at, "dt"))
                at.enter("prep", lay)
                for j in range(2):
                    pe.wait_ge(*hn_ready.after(at, ("m", j), "first", 0))
                    for kk in range(2):
                        turns(5 + (2 * j + kk) % 3, [hn[:, PT + j, (4 * kk + n) * P:(4 * kk + n + 1) * P] for n in range(4)], ("m", j, kk))
                for q in (1, 3):
                    channel_slab("XS", 0, q)
                pe.wait_ge(*split_lo.after(at, "m"))
                pe.wait_ge(*dve_s.after(at, "da"))
                use(4)
                f, bw = (da[:, d, :, :].rearrange("p c h -> p (c h)") for d in range(2))
                nc.tensor.matmul(bank[4][:, 0:P], cst[:, LE, :], f, start=True, stop=True)
                nc.tensor.matmul(bank[4][:, P:2 * P], cst[:, GE, :], bw, start=True, stop=True)
                nc.tensor.matmul(bank[4][:, 2 * P:3 * P], cst[:, GT, :], f, start=True, stop=True)
                nc.tensor.matmul(bank[4][:, 3 * P:4 * P], cst[:, LT, :], bw, start=True, stop=True)\
                    .then_inc(*full[4].tick(at, "cum"))
                use(5)
                nc.tensor.matmul(bank[5][:, 0:2 * P], cst[:, ONES, :], da[:].rearrange("p d c h -> p (d c h)"),
                                 start=True, stop=True).then_inc(*full[5].tick(at, "tot"))

                def step_in(i):
                    use(5)
                    c = slice(i * P, (i + 1) * P)
                    nc.tensor.matmul(bank[5][:, 0:P], bct[:, 0, c], bct[:, 1, c], start=True, stop=True)\
                        .then_inc(*full[5].tick(at, ("cb", i)))
                    pe.wait_ge(*bnd_ready.after(at, i))
                    use(6)
                    for d, mask in ((0, GT), (1, LT)):
                        for n in range(2):
                            mm = nc.tensor.matmul(bank[6][:], mask16[:, mask - LE, :],
                                                  bnd[:, i % 2, d, n].rearrange("p h l -> p (h l)"),
                                                  start=d == 0 and n == 0, stop=d == 1 and n == 1)
                    mm.then_inc(*full[6].tick(at, ("seg", i)))

                def step_out(i):
                    j = PT - 1 - i
                    ci, cj = slice(i * P, (i + 1) * P), slice(j * P, (j + 1) * P)
                    pe.wait_ge(*x_ready.after(at, i))
                    pe.wait_ge(*s_ready[0].after(at, i))
                    use(5)
                    nc.tensor.matmul(bank[5][:, 0:COLS], b_p[:, i, :], xw[:, i % 2, 0].rearrange("p h d -> p (h d)"),
                                     start=True, stop=True).then_inc(*full[5].tick(at, ("st", i)))
                    pe.wait_ge(*s_ready[1].after(at, i))
                    use(4)
                    nc.tensor.matmul(bank[4][:, 0:COLS], bct[:, 1, cj], S[:, 1].rearrange("p h d -> p (h d)"),
                                     start=True, stop=True)
                    nc.tensor.matmul(bank[4][:, COLS:HALF], b_p[:, j, :], xw[:, i % 2, 1].rearrange("p h d -> p (h d)"),
                                     start=True, stop=True).then_inc(*full[4].tick(at, ("bw", i)))
                    pe.wait_ge(*m_ready.after(at, i))
                    use(7)
                    nc.tensor.matmul(bank[7][:, COLS:HALF], bct[:, 1, ci], S[:, 0].rearrange("p h d -> p (h d)"),
                                     start=True, stop=True)
                    for h in range(HG):
                        mm = nc.tensor.matmul(bank[7][:, h * HD:(h + 1) * HD], Mx[:, h, :], xs_p[:, i, h * HD:(h + 1) * HD],
                                              start=True, stop=True)
                    mm.then_inc(*full[7].tick(at, ("in", i)))

                def scores(j):
                    use(4)
                    if j == 0:
                        pe.wait_ge(*free[1].after(at, ("QM", 1)))
                    for n in range(2):
                        t = 2 * j + n
                        mm = nc.tensor.matmul(bank[4][:, n * M:(n + 1) * M], qT[:, t * P:(t + 1) * P], kT[:],
                                              start=True, stop=True)
                    mm.then_inc(*full[4].tick(at, ("sc", j)))

                def probs_turn(j):
                    pe.wait_ge(*dve_s.after(at, ("pr", j)))
                    turns(6, [probs[:, j, n, m * P:(m + 1) * P] for n in range(2) for m in range(2)], ("pt", j))

                with pe.Fori(0, G) as g:
                    at.enter("group", lay, g)
                    for q in range(4):
                        channel_slab("BC", 1, q)
                    slab_ready(0)
                    use(4)
                    products(bank[4][:, 0:M], lambda a, k: w16[:, 0, a, k, 0:P], lambda b, k: memT[:, b, k, :], range(KT))\
                        .then_inc(*full[4].tick(at, "k"))
                    use(5)
                    for m in range(2):
                        mm = products(bank[5][:, m * P:(m + 1) * P], lambda a, k: memT[:, a, k, m * P:(m + 1) * P],
                                      lambda b, k: w16[:, 0, b, k, P:2 * P], range(KT))
                    mm.then_inc(*full[5].tick(at, "v"))
                    pe.wait_ge(*silu_done.after(at, "x1"))
                    for n in (2, 3, 0, 1):
                        turns(4 + n, [cv[:, blk, t * P:(t + 1) * P] for t in (2 * n, 2 * n + 1) for blk in range(2)], ("tx", n))
                    for q in range(4):
                        channel_slab("UF", 1, q)
                    pe.wait_ge(*silu_done.after(at, "B"))
                    for n in range(2):
                        turns(4 + n, [bct[:, 0, t * P:(t + 1) * P] for t in range(4 * n, 4 * n + 4)], ("tb", n))
                    pe.wait_ge(*dve_s.after(at, "fold"))
                    for n, (b, table) in enumerate(((6, COSC), (7, SINC))):
                        use(b)
                        for t in range(4):
                            mm = nc.tensor.matmul(bank[b][:, t * P:(t + 1) * P], uf[:, n, t * P:(t + 1) * P], cst[:, table, :],
                                                  start=True, stop=True)
                        mm.then_inc(*full[b].tick(at, ("dftc", n)))
                    use(4)
                    nc.tensor.matmul(bank[4][0:1, 0:P], eo[:, 0, COLS:COLS + 1], cst[:, COSC, :], start=True, stop=True)\
                        .then_inc(*full[4].tick(at, "ny"))
                    channel_slab("QM", 0, 0)
                    pe.wait_ge(*silu_done.after(at, "C"))
                    step_in(0)
                    pe.wait_ge(*dft_in_s.reached(dft_in_s.begin(at)))
                    pe.wait_ge(*split_lo.after(at, "ny"))
                    pe.wait_ge(*free[5].after(at, ("tb", 1)))

                    def dense(i, part):
                        def over_positions(n, b):
                            for odd in range(2):
                                mm = products(bank[b][:, odd * COLS:(odd + 1) * COLS], lambda a, t: pq16[:, n, a, t * P:(t + 1) * P],
                                              lambda c, t: dft[:, n, c, t, :], range(2 * odd, 2 * odd + 2), last=n == 1 or odd == 1)
                                if n == 0 and odd == 0:
                                    for a in range(2):
                                        mm = nc.tensor.matmul(bank[b][:, 0:COLS], ny16[0:1, a, :], altr[:], start=False, stop=a == 1)
                            return mm

                        if i == 0 and part == 0:
                            use(3)
                            over_positions(0, 3).then_inc(*full[3].tick(at, "cos"))
                        elif i == 0:
                            use(2)
                            over_positions(1, 2).then_inc(*full[2].tick(at, "sin"))
                            use(0)
                            for t in range(2):
                                for a in range(2):
                                    nc.tensor.matmul(bank[0][:, 0:1], pq16[:, 0, a, t * P:(t + 1) * P], altc[:, 0:1],
                                                     start=t == 0 and a == 0, stop=False)
                            for a in range(2):
                                mm = nc.tensor.matmul(bank[0][:, 0:1], ny16[0:1, a, :], altc[0:1, 0:1], start=False, stop=a == 1)
                            mm.then_inc(*full[0].tick(at, "mid"))
                        elif i < 4:
                            channel_slab("QM", 0, i, parts=(part,))
                        else:
                            position_slab("Z", 1, i - 4, hT, parts=(part,))

                    for i in range(PT):
                        dense(i, 0)
                        if 3 <= i < 7:
                            scores(i - 3)
                        if i < PT - 1:
                            step_in(i + 1)
                        dense(i, 1)
                        if i >= 4:
                            probs_turn(i - 4)
                        step_out(i)
                    channel_slab("NX", 0, 0)
                    pe.wait_ge(*free[6].after(at, ("pt", 3)))
                    for half in range(2):
                        use(6 + half)
                        for m in range(2):
                            mm = nc.tensor.matmul(bank[6 + half][:], vM[:, m, :], pT[:, m, half * HALF:(half + 1) * HALF],
                                                  start=m == 0, stop=m == 1)
                        mm.then_inc(*full[6 + half].tick(at, ("pv", half)))
                    for q in range(1, 4):
                        channel_slab("NX", 0, q)
                    pe.wait_ge(*dve_s.after(at, "yn"))
                    for n, (blk, half) in enumerate(((0, 0), (0, 1), (1, 0), (1, 1))):
                        turns(4 + n, [Y[:, t, blk * P:(blk + 1) * P] for t in range(4 * half, 4 * half + 4)], ("ty", n))

                at.enter("merge", lay)
                for j in range(4):
                    p0 = j % 2
                    if j > 0:
                        for q in range(4):
                            channel_slab(f"G0{j}", p0, q)
                    for q in range(4):
                        channel_slab(f"G1{j}", 1 - p0, q)
                    if j == 0:
                        pe.wait_ge(*y_back[0].reached(y_back[0].begin(at)))
                    for q in range(4):
                        channel_slab(f"PS{j}", p0, q, lambda c, k: yT[:, k, c, :])
                    for q in range(4):
                        channel_slab(f"G2{j}", 1 - p0, q)
                    if j == 0:
                        pe.wait_ge(*y_back[1].reached(y_back[1].begin(at)))
                    slab_ready(p0)
                    for name, kts in (("F", range(0, 4)), ("M", range(4, 8))):
                        for q in range(4):
                            use(q)
                            channel_tile(q, p0, q // 2, q % 2, lambda c, k: yT[:, 8 + k, c, :], kts)\
                                .then_inc(*full[q].tick(at, (f"P{name}{j}", q)))
                at.enter("out", lay)
                pe.wait_ge(*m_lo.after(at, (2, 3), "merge", 0))
                slab_ready(0)

                def first_slab(q, j, kts, **ends):
                    pt = 2 * q + j
                    return products(bank[q][:, j * COLS:(j + 1) * COLS], lambda a, k: mT[:, a, k, pt * P:(pt + 1) * P],
                                    lambda b, k: w16[:, 0, b, k, :], kts, **ends)

                for q in range(4):
                    use(q)
                    first_slab(q, 0, range(6), last=False)
                pe.wait_ge(*m_lo.after(at, (3, 3), "merge", 0))
                for q in range(4):
                    first_slab(q, 0, range(6, KT), first=False)
                    first_slab(q, 1, range(KT)).then_inc(*full[q].tick(at, ("O0", q)))
                for s, name in list(enumerate(OUT_SLABS))[1:]:
                    for q in range(4):
                        position_slab(name, s % 2, q, mT)

        @block.scalar
        def _(act):
            at = At()
            at.enter("pre")

            def fill(slot):
                act.wait_ge(*raw_in[slot].reached(w_hi[slot].count(at) + 1))
                nc.scalar.activation(w16[:, slot, 0].rearrange("p k n -> p (k n)"), raw[:, slot, :], ACT.Copy, scale=WS)\
                    .then_inc(*w_hi[slot].tick(at))

            def tanh(dst, src, scale, key, waits=True):
                if waits:
                    act.wait_ge(*th_used.reached(th_ready.count(at)))
                nc.scalar.activation(dst, src, ACT.Tanh, scale=scale).then_inc(*th_ready.tick(at, key))

            def send_out(r, src, key):
                act.wait_ge(*spill[r].reached(o_hi[r].count(at)))
                nc.scalar.activation(place[r][:, 0, :], src, ACT.Copy).then_inc(*o_hi[r].tick(at, key))

            def link(op):
                op.then_inc(*act_chain.tick(at))
                act.wait_ge(*act_chain.now(at))

            def squares(n, scrap, src, last=None):
                op = nc.scalar.activation(scrap, src, ACT.Square, accum_out=rs[:, n:n + 1])
                if last:
                    op.then_inc(*act_s.tick(at, last))
                else:
                    link(op)

            def pre_copy(name, q, phase=None):
                copy_bank(q, (name, q), pre[:, q // 2, 2 + (q % 2) * HALF:2 + (q % 2 + 1) * HALF], bank[q][:], 0.5 / WS, phase)

            def copy_bank(b, key, dst, src, scale, phase=None):
                act.wait_ge(*full[b].after(at, key, phase))
                nc.scalar.activation(dst, src, ACT.Copy, scale=scale).then_inc(*free[b].tick(at, key))

            act.wait_ge(*start_in.reached(1))

            def half_rms(half, parts=()):
                for t in range(4 * half, 4 * half + 4):
                    if parts and t % 2 == 0:
                        act.wait_ge(*parts[t % 4 // 2])
                    squares(t, junk[:], X[:, t, :], ("ss", half) if t % 4 == 3 else None)
                act.wait_ge(*dve_s.after(at, ("var", half)))
                cols = slice(4 * half, 4 * half + 4)
                nc.scalar.activation(rr[:, cols], rs[:, cols], ACT.Sqrt).then_inc(*act_s.tick(at, ("rms", half)))

            for half in range(2):
                act.wait_ge(*x_in_s[half].reached(1))
                half_rms(half)
            with act.Fori(0, DEPTH) as lay:
                at.enter("head", lay)
                fill(0)
                at.enter("norm", lay)
                for t in range(PT):
                    for kk in range(2):
                        b = 2 * (t % 4) + kk
                        act.wait_ge(*full[b].after(at, ("h", t, kk)))
                        nc.scalar.activation(hT[:, 0, 4 * kk:4 * kk + 4, t * P:(t + 1) * P],
                                             bank[b][:].rearrange("p (k l) -> p k l", k=4), ACT.Copy)\
                            .then_inc(*split_hi.tick(at, (t, kk)))
                at.enter("first", lay)
                act.wait_ge(*mem_in_s.reached(mem_in_s.begin(at, "norm")))
                for n in range(2):
                    squares(PT + n, junk[:], memX[:, n, :], ("ss", "m") if n else None)
                act.wait_ge(*dve_s.after(at, ("var", "m")))
                nc.scalar.activation(rr[:, PT:PT + 2], rs[:, PT:PT + 2], ACT.Sqrt).then_inc(*act_s.tick(at, ("rms", "m")))
                at.enter("prep", lay)
                for j in range(2):
                    for kk in range(2):
                        b = 5 + (2 * j + kk) % 3
                        act.wait_ge(*full[b].after(at, ("m", j, kk)))
                        nc.scalar.activation(memT[:, 0, 4 * kk:4 * kk + 4, j * P:(j + 1) * P],
                                             bank[b][:].rearrange("p (k l) -> p k l", k=4), ACT.Copy)\
                            .then_inc(*split_hi.tick(at, (j, kk)))
                fill(1)
                act.wait_ge(*dve_s.after(at, "abs"))
                nc.scalar.activation(sp_t[:, 1, :], sp_t[:, 1, :], ACT.Exp).then_inc(*act_s.tick(at, "exp"))
                nc.scalar.activation(par[:, ALOG:ALOG + 32], par[:, ALOG:ALOG + 32], ACT.Exp).then_inc(*act_s.tick(at, "A"))
                act.wait_ge(*dve_s.after(at, "1+exp"))
                nc.scalar.activation(sp_t[:, 3, :], sp_t[:, 2, :], ACT.Ln).then_inc(*act_s.tick(at, "ln"))
                act.wait_ge(*full[4].after(at, "cum"))
                nc.scalar.activation(ea[:].rearrange("p d c h -> p (d c h)"), bank[4][:, 0:2 * P], ACT.Exp)
                nc.scalar.activation(sp_t[:, 0, :], bank[4][:, 2 * P:4 * P], ACT.Exp).then_inc(*free[4].tick(at, "cum"))
                act.wait_ge(*full[5].after(at, "tot"))
                nc.scalar.activation(tot[:].rearrange("p d c h -> p (d c h)"), bank[5][:, 0:2 * P], ACT.Exp)\
                    .then_inc(*free[5].tick(at, "tot"))
                act.wait_ge(*x_saved.reached(x_saved.begin(at)))
                for q in range(4):
                    pre_copy("XS", q, "prep" if q % 2 else "first")
                fill(0)
                act.wait_ge(*dve_s.after(at, "prep"))

                with act.Fori(0, G) as g:
                    at.enter("group", lay, g)

                    def conv_tanh(key, src):
                        act.wait_ge(*conv_done.after(at, key))
                        tanh(th[:], src[:, 0:HALF], 1.0, (key, 0))
                        tanh(E[:].rearrange("p h l -> p (h l)"), src[:, HALF:L], 1.0, (key, 1), waits=False)

                    act.wait_ge(*spill[3].reached(spill[3].begin(at)))
                    conv_tanh("x0", cv[:, 0, :])
                    for q in (0, 1):
                        pre_copy("BC", q)
                    act.wait_ge(*full[3].after(at, ("BC", 3)))
                    fill(1)
                    conv_tanh("x1", cv[:, 1, :])
                    for q in (2, 3):
                        pre_copy("BC", q)
                    copy_bank(4, "k", kT[:], bank[4][:, 0:M], 1 / WS)
                    copy_bank(5, "v", vM[:].rearrange("p m d -> p (m d)"), bank[5][:, 0:2 * P], 1 / WS)
                    conv_tanh("B", bct[:, 0, :])
                    for n in (2, 3, 0, 1):
                        copy_bank(4 + n, ("tx", n), xs_p[:, 2 * n:2 * n + 2, :].rearrange("p t c -> p (t c)"), bank[4 + n][:], 1.0)
                    fill(0)
                    conv_tanh("C", bct[:, 1, :])
                    copy_bank(0, ("UF", 0), uT[:, 0:HALF], bank[0][:], 1 / WS)
                    copy_bank(1, ("UF", 1), uT[:, HALF:L], bank[1][:], 1 / WS)
                    for q in (2, 3):
                        act.wait_ge(*full[q].after(at, ("UF", q)))
                        tanh(th[:], bank[q][:], 0.5 / WS, ("UF", q))
                    for n in range(2):
                        copy_bank(4 + n, ("tb", n), b_p[:, 4 * n:4 * n + 4, :].rearrange("p t c -> p (t c)"), bank[4 + n][:], 1.0)
                    for n in range(2):
                        act.wait_ge(*full[6 + n].after(at, ("dftc", n)))
                        nc.scalar.activation(pq16[:, n, 0, :], bank[6 + n][:], ACT.Copy).then_inc(*split_hi.tick(at, ("dftc", n)))
                    act.wait_ge(*full[4].after(at, "ny"))
                    nc.scalar.activation(ny16[:, 0, :], bank[4][0:1, 0:P], ACT.Copy).then_inc(*split_hi.tick(at, "ny"))
                    fill(1)
                    copy_bank(0, ("QM", 0), qT[:, 0:HALF], bank[0][:], 1 / WS)

                    def decays(i):
                        act.wait_ge(*full[6].after(at, ("seg", i)))
                        if i >= 1:
                            act.wait_ge(*m_ready.after(at, i - 1))
                        nc.scalar.activation(E[:].rearrange("p h l -> p (h l)"), bank[6][:], ACT.Exp)\
                            .then_inc(*free[6].tick(at, ("seg", i)))

                    decays(0)
                    for i in range(PT):
                        if 3 <= i < 7:
                            j = i - 3
                            act.wait_ge(*dve_s.after(at, ("max", j)))
                            for n in range(2):
                                op = nc.scalar.activation(probs[:, j, n, :], bank[4][:, n * M:(n + 1) * M], ACT.Exp,
                                                          bias=att[:, 0, n:n + 1], scale=float(P) ** -0.5,
                                                          accum_out=att[:, 1, n:n + 1])
                            op.then_inc(*free[4].tick(at, ("sc", j)))
                        if i < PT - 1:
                            decays(i + 1)
                        if i == 0:
                            copy_bank(2, "sin", qs[:], bank[2][:], 1.0)
                        elif i == 1:
                            copy_bank(1, ("QM", 1), qT[:, HALF:L], bank[1][:], 1 / WS)
                            for half in range(2):
                                act.wait_ge(*o_in.after(at, ("f", half)))
                                send_out(half, yf[:, half * HALF:(half + 1) * HALF], ("f", half))
                        elif i < 4:
                            act.wait_ge(*full[i].after(at, ("QM", i)))
                            tanh(th[:], bank[i][:], 0.5 / WS, ("QM", i))
                        else:
                            act.wait_ge(*full[i - 4].after(at, ("Z", i - 4)))
                            tanh(th[:], bank[i - 4][:], 0.5 / WS, ("Z", i - 4))
                        if i in (3, 7):
                            fill(i // 4)
                        if i >= 4:
                            j = i - 4
                            copy_bank(6, ("pt", j), pT[:, :, 2 * j * P:(2 * j + 2) * P].rearrange("p m (n l) -> p n m l", n=2),
                                      bank[6][:].rearrange("p (n m l) -> p n m l", n=2, m=2), 1.0)
                    for t in range(PT):
                        act.wait_ge(*dve_s.after(at, ("yg", t // 2)))
                        squares(t, E[:].rearrange("p h l -> p (h l)")[:, 0:COLS], Y[:, t, :], ("ss", 0) if t == PT - 1 else None)
                    act.wait_ge(*dve_s.after(at, ("var", 0)))
                    nc.scalar.activation(rr[:, 0:PT], rs[:, 0:PT], ACT.Sqrt).then_inc(*act_s.tick(at, ("rms", 0)))
                    for half in range(2):
                        act.wait_ge(*o_in.after(at, ("m", half)))
                        send_out(half, qs[:], ("m", half))
                    for q in range(4):
                        pre_copy("NX", q)
                    fill(0)
                    for n in range(4):
                        act.wait_ge(*full[4 + n].after(at, ("ty", n)))
                        send_out((2, 3, 0, 1)[n], bank[4 + n][:], ("s", n))

                at.enter("merge", lay)
                for q in range(4):
                    act.wait_ge(*t_used.reached(tanhs.count(at) + (1 - 8)))
                    act.wait_ge(*free[q].reached(free[q].begin(at)))
                    tanhs.tick(at)
                    nc.scalar.activation(tg[:, 0, q, :], pre[:, q // 2, 2 + (q % 2) * HALF:2 + (q % 2 + 1) * HALF], ACT.Tanh)\
                        .then_inc(*act_s.tick(at, ("g0", q)))
                for j in range(4):
                    for b in range(j == 0, 3):
                        name = f"G{b}{j}"
                        slot = (j + (0, 1, 1)[b]) % 2
                        for q in range(4):
                            act.wait_ge(*full[q].after(at, (name, q)))
                            act.wait_ge(*t_used.reached(tanhs.count(at) + (1 - 8)))
                            tanhs.tick(at)
                            op = nc.scalar.activation(tg[:, (3 * j + b) % 2, q, :], bank[q][:], ACT.Tanh, scale=0.5 / WS)
                            op.then_inc(*free[q].tick(at, (name, q)))
                            if q == 0 and (j, b) != (0, 1):
                                fill(1 - slot)
                        if b == 1:
                            act.wait_ge(*full[0].after(at, (f"PS{j}", 0)))
                            fill(slot)
                    act.wait_ge(*full[0].after(at, (f"PF{j}", 0)))
                    fill(1 - j % 2)
                    for q in range(4):
                        act.wait_ge(*m_in.after(at, (j, q)))
                        nc.scalar.activation(mT[:, 0, 2 * j + q // 2, (q % 2) * HALF:(q % 2 + 1) * HALF],
                                             acc[:, q, :], ACT.Copy, scale=0.5 / WS).then_inc(*m_hi.tick(at, (j, q)))
                at.enter("out", lay)
                for s in range(3):
                    act.wait_ge(*full[0].after(at, (OUT_SLABS[s], 0)))
                    fill(1 - s % 2)
                for half in range(2):
                    half_rms(half, [free[q].after(at, ("O3", q)) for q in (2 * half, 2 * half + 1)])

        @block.vector
        def _(dve):
            at = At()
            at.enter("pre")
            V = nc.vector
            for one in lines:
                if one.opened:
                    dve.sem_inc(one.sem, one.opened * one.step)

            def link(op):
                op.then_inc(*chain.tick(at))
                dve.wait_ge(*chain.now(at))

            def settle(one):
                dve.wait_ge(*one.now(at))

            def split_slab(slot):
                dve.wait_ge(*w_hi[slot].reached(w_lo[slot].count(at) + 1))
                V.scalar_tensor_tensor(w16[:, slot, 1].rearrange("p k n -> p (k n)"), raw[:, slot, :], WS,
                                       w16[:, slot, 0].rearrange("p k n -> p (k n)"), ALU.mult, ALU.subtract)\
                    .then_inc(*w_lo[slot].tick(at))

            def inverse_rms(cols, width, which=0):
                dve.wait_ge(*act_s.after(at, ("ss", which)))
                V.tensor_scalar(rs[:, cols], rs[:, cols], 1.0 / width, EPS, ALU.mult, ALU.add)\
                    .then_inc(*dve_s.tick(at, ("var", which)))
                dve.wait_ge(*act_s.after(at, ("rms", which)))
                V.reciprocal(rr[:, cols], rr[:, cols]).then_inc(*dve_s.tick(at, ("rr", which)))

            def normalise(t):
                V.scalar_tensor_tensor(hn[:, t, :], X[:, t, :], rr[:, t:t + 1], grow[:, 0, :], ALU.mult, ALU.mult)\
                    .then_inc(*hn_ready.tick(at, ("h", t)))

            def half_rms(half):
                inverse_rms(slice(4 * half, 4 * half + 4), D, half)
                if half == 0:
                    settle(dve_s)
                    dve.wait_ge(*gain_in.reached(gain_in.begin(at) + 1))
                    for t in range(4):
                        normalise(t)

            dve.wait_ge(*start_in.reached(1))
            link(V.tensor_copy(mask16[:], cst[:, LE:LT + 1, :]))
            for half in range(2):
                half_rms(half)
            with dve.Fori(0, DEPTH) as lay:
                at.enter("head", lay)
                def lo_part(dst, b, key, hi, freed):
                    dve.wait_ge(*split_hi.after(at, key))
                    V.tensor_tensor(dst, bank[b][:].rearrange("p (k l) -> p k l", k=4), hi, ALU.subtract)\
                        .then_inc(*free[b].tick(at, freed))

                at.enter("norm", lay)
                dve.wait_ge(*dve_s.reached(dve_s.begin(at, "head")))
                for t in range(4, PT + 4):
                    if t < PT:
                        normalise(t)
                    if t == PT + 1:
                        dve.wait_ge(*free[7].after(at, ("h", 3, 1)))
                        dve.sem_inc(*split_lo.tick(at, "half h"))
                        split_slab(0)
                    at_l = slice((t - 4) * P, (t - 3) * P)
                    for kk in range(2):
                        lo_part(hT[:, 1, 4 * kk:4 * kk + 4, at_l], 2 * (t % 4) + kk, (t - 4, kk),
                                hT[:, 0, 4 * kk:4 * kk + 4, at_l], ("h", t - 4, kk))
                at.enter("first", lay)
                dve.wait_ge(*free[7].after(at, ("h", PT - 1, 1), "norm", 0))
                dve.sem_inc(*split_lo.tick(at, "h"))
                dve.wait_ge(*par_in_s.reached(par_in_s.begin(at, "norm")))
                link(V.tensor_scalar(wdt[:, 0].rearrange("p k n -> p (k n)"), wdt_raw[:], WS, None, ALU.mult))
                V.scalar_tensor_tensor(wdt[:, 1].rearrange("p k n -> p (k n)"), wdt_raw[:], WS,
                                       wdt[:, 0].rearrange("p k n -> p (k n)"), ALU.mult, ALU.subtract)\
                    .then_inc(*dve_s.tick(at, "wdt"))
                link(V.tensor_scalar(par[:, CB:CB + 16], par[:, CB:CB + 16], 0.5, None, ALU.mult))
                inverse_rms(slice(PT, PT + 2), D, "m")
                dve.wait_ge(*mem_in_s.reached(mem_in_s.begin(at)))
                dve.wait_ge(*dve_s.after(at, ("rr", "m")))
                for j in range(2):
                    V.scalar_tensor_tensor(hn[:, PT + j, :], memX[:, j, :], rr[:, PT + j:PT + j + 1], grow[:, 1, :],
                                           ALU.mult, ALU.mult).then_inc(*hn_ready.tick(at, ("m", j)))
                dve.wait_ge(*full[4].after(at, "dt"))
                for d in range(2):
                    op = V.scalar_tensor_tensor(dt_[:, d], bank[4][:, 0:2 * P].rearrange("p (c d h) -> p d c h", c=PT, d=2)[:, d], 1 / WS,
                                                par[:, DTB + d * NH:DTB + (d + 1) * NH].unsqueeze(1).to_broadcast([P, PT, NH]),
                                                ALU.mult, ALU.add)
                op.then_inc(*free[4].tick(at, "dt"))
                at.enter("prep", lay)
                for j in range(2):
                    for kk in range(2):
                        lo_part(memT[:, 1, 4 * kk:4 * kk + 4, j * P:(j + 1) * P], 5 + (2 * j + kk) % 3, (j, kk),
                                memT[:, 0, 4 * kk:4 * kk + 4, j * P:(j + 1) * P], ("m", j, kk))
                dve.wait_ge(*free[5].after(at, ("m", 1, 1)))
                dve.sem_inc(*split_lo.tick(at, "m"))
                split_slab(1)
                dve.wait_ge(*free[4].after(at, "dt", "first", 0))
                v = dt_[:].rearrange("p d c h -> p (d c h)")
                V.scalar_tensor_tensor(sp_t[:, 1, :], v, -1.0, v, ALU.mult, ALU.min).then_inc(*dve_s.tick(at, "abs"))
                dve.wait_ge(*act_s.after(at, "A"))
                V.tensor_scalar(sp_t[:, 2, :], sp_t[:, 1, :], 1.0, None, ALU.add).then_inc(*dve_s.tick(at, "1+exp"))
                settle(dve_s)
                link(V.tensor_scalar(sp_t[:, 4, :], sp_t[:, 2, :], -1.0, None, ALU.add))
                link(V.tensor_scalar(sp_t[:, 5, :], sp_t[:, 4, :], 0.0, None, ALU.is_equal))
                link(V.tensor_tensor(sp_t[:, 4, :], sp_t[:, 4, :], sp_t[:, 5, :], ALU.add))
                link(V.reciprocal(sp_t[:, 4, :], sp_t[:, 4, :]))
                dve.wait_ge(*act_s.after(at, "ln"))
                link(V.tensor_tensor(sp_t[:, 3, :], sp_t[:, 3, :], sp_t[:, 5, :], ALU.add))
                link(V.tensor_tensor(sp_t[:, 3, :], sp_t[:, 3, :], sp_t[:, 4, :], ALU.mult))
                link(V.tensor_tensor(sp_t[:, 3, :], sp_t[:, 3, :], sp_t[:, 1, :], ALU.mult))
                link(V.scalar_tensor_tensor(v, v, 0.0, sp_t[:, 3, :], ALU.max, ALU.add))
                A = par[:, ALOG:ALOG + 32].rearrange("p (d h) -> p d h", d=2)
                for d in range(2):
                    op = V.scalar_tensor_tensor(da[:, d], dt_[:, d], -1.0, A[:, d].unsqueeze(1).to_broadcast([P, PT, NH]),
                                                ALU.mult, ALU.mult)
                op.then_inc(*dve_s.tick(at, "da"))
                dve.wait_ge(*free[4].after(at, "cum"))
                link(V.tensor_tensor(dd[:].rearrange("p d c h -> p (d c h)"), v, sp_t[:, 0, :], ALU.mult))
                dve.wait_ge(*free[5].after(at, "tot"))
                dve.wait_ge(*x_saved.reached(x_saved.begin(at)))
                for b in range(2):
                    V.memset(pre[:, b, 0:2], 0.0)
                    op = V.memset(pre[:, b, L + 2:L + 4], 0.0)
                op.then_inc(*dve_s.tick(at, "prep"))
                split_slab(0)

                with dve.Fori(0, G) as g:
                    at.enter("group", lay, g)

                    def silu(dst, src, tanh_of, key, waits=True):
                        dve.wait_ge(*th_ready.after(at, key))
                        return V.scalar_tensor_tensor(dst, tanh_of, 1.0, src, ALU.add, ALU.mult)

                    def gate(q, key, dst):
                        silu(dst, bank[q][:], th[:], (key, q)).then_inc(*free[q].tick(at, (key, q)))
                        dve.wait_ge(*free[q].after(at, (key, q)))
                        dve.sem_inc(*th_used.tick(at, (key, q)))

                    def conv(key, blk, dst, n):
                        q = 2 * blk + 1
                        dve.wait_ge(*(free[q].reached(free[q].begin(at)) if n < 2 else free[q].after(at, ("BC", q))))
                        link(V.tensor_scalar(dst, pre[:, blk, 0:L], gcw[:, n, 0:1], gcb[:, n:n + 1], ALU.mult, ALU.add))
                        for k in range(1, 5):
                            op = V.scalar_tensor_tensor(dst, pre[:, blk, k:k + L], gcw[:, n, k:k + 1], dst, ALU.mult, ALU.add)
                            if k < 4:
                                link(op)
                        op.then_inc(*conv_done.tick(at, key))

                    def conv_silu(key, dst):
                        dve.wait_ge(*conv_done.after(at, key))
                        silu(dst[:, 0:HALF], dst[:, 0:HALF], th[:], (key, 0)).then_inc(*th_used.tick(at, (key, 0)))
                        silu(dst[:, HALF:L], dst[:, HALF:L], E[:].rearrange("p h l -> p (h l)"), (key, 1))\
                            .then_inc(*th_used.tick(at, (key, 1)))
                        dve.wait_ge(*th_used.now(at))
                        dve.sem_inc(*silu_done.tick(at, key))

                    V.tensor_copy(gcw[:].rearrange("p b k -> p (b k)"), par[:, bass.ds(g * 20 + CW, 20)])
                    V.tensor_copy(gcb[:], par[:, bass.ds(g * 4 + CB, 4)])
                    V.tensor_copy(gdk[:], par[:, bass.ds(g * HG + DSK, HG)])
                    for dst, src in ((gdt, dt_), (gea, ea), (gdd, dd), (gtot, tot)):
                        V.tensor_copy(dst[:].rearrange("p d c h -> p (d c) h"),
                                      src[:].rearrange("p d c h -> p (d c) h")[:, :, bass.ds(g * HG, HG)])
                    da_g = da[:].rearrange("p d c h -> p (d c) h")[:, :, bass.ds(g * HG, HG)]
                    hi, lo = (gda[:, n].rearrange("p d c h -> p (d c) h") for n in range(2))
                    link(V.tensor_copy(hi, da_g))
                    V.tensor_tensor(lo, da_g, hi, ALU.subtract)
                    V.memset(S[:, 0].rearrange("p h d -> p (h d)"), 0.0).then_inc(*s_ready[0].tick(at, 0))
                    V.memset(S[:, 1].rearrange("p h d -> p (h d)"), 0.0).then_inc(*s_ready[1].tick(at, 0))
                    settle(s_ready[1])
                    dve.sem_inc(*dve_s.tick(at, "gc"))
                    conv("x0", 0, cv[:, 0, :], 0)
                    conv("x1", 1, cv[:, 1, :], 1)
                    conv_silu("x0", cv[:, 0, :])
                    split_slab(1)
                    conv_silu("x1", cv[:, 1, :])
                    conv("B", 0, bct[:, 0, :], 2)
                    conv_silu("B", bct[:, 0, :])
                    conv("C", 1, bct[:, 1, :], 3)
                    split_slab(0)
                    conv_silu("C", bct[:, 1, :])
                    dve.wait_ge(*free[1].after(at, ("UF", 1)))
                    V.tensor_tensor(eo[:, 0, 1:HALF], uT[:, 1:HALF], uT[:, L - 1:HALF:-1], ALU.add)
                    V.tensor_tensor(eo[:, 1, 1:HALF], uT[:, 1:HALF], uT[:, L - 1:HALF:-1], ALU.subtract)
                    link(V.tensor_copy(eo[:, 0, 0:HALF + 1:HALF], uT[:, 0:HALF + 1:HALF]))
                    ev, od, Q2 = eo[:, 0], eo[:, 1], COLS
                    V.tensor_tensor(uf[:, 0, 0:Q2], ev[:, 0:Q2], ev[:, HALF:Q2:-1], ALU.add)
                    V.tensor_tensor(uf[:, 0, Q2:HALF], ev[:, 0:Q2], ev[:, HALF:Q2:-1], ALU.subtract)
                    V.tensor_tensor(uf[:, 1, 1:Q2], od[:, 1:Q2], od[:, HALF - 1:Q2:-1], ALU.subtract)
                    V.tensor_tensor(uf[:, 1, Q2 + 1:HALF], od[:, 1:Q2], od[:, HALF - 1:Q2:-1], ALU.add)
                    V.tensor_copy(uf[:, 1, Q2:Q2 + 1], od[:, Q2:Q2 + 1])
                    V.memset(uf[:, 1, 0:1], 0.0).then_inc(*dve_s.tick(at, "fold"))
                    for q in (2, 3):
                        gate(q, "UF", zg[:, (q - 2) * HALF:(q - 1) * HALF])
                    for n in range(2):
                        dve.wait_ge(*split_hi.after(at, ("dftc", n)))
                        V.tensor_tensor(pq16[:, n, 1, :], bank[6 + n][:], pq16[:, n, 0, :], ALU.subtract)\
                            .then_inc(*free[6 + n].tick(at, ("dftc", n)))
                    dve.wait_ge(*split_hi.after(at, "ny"))
                    V.tensor_tensor(ny16[:, 1, :], bank[4][0:1, 0:P], ny16[:, 0, :], ALU.subtract)\
                        .then_inc(*free[4].tick(at, "ny"))
                    dve.wait_ge(*free[4].after(at, "ny"))
                    dve.sem_inc(*split_lo.tick(at, "ny"))

                    def spectrum():
                        dve.wait_ge(*full[3].after(at, "cos"))
                        dve.wait_ge(*free[2].after(at, "sin"))
                        V.tensor_tensor(yf[:, 0:HALF].rearrange("p (m e) -> p e m", e=2), bank[3][:].rearrange("p (e m) -> p e m", e=2),
                                        qs[:].rearrange("p (e m) -> p e m", e=2), ALU.subtract)
                        V.tensor_tensor(yf[:, L - 2:HALF:-2], bank[3][:, 1:COLS], qs[:, 1:COLS], ALU.add)
                        V.tensor_tensor(yf[:, L - 1:HALF:-2], bank[3][:, COLS:HALF], qs[:, COLS:HALF], ALU.add)\
                            .then_inc(*free[3].tick(at, "cos"))
                        dve.wait_ge(*full[0].after(at, "mid"))
                        V.tensor_copy(yf[:, HALF:HALF + 1], bank[0][:, 0:1]).then_inc(*free[0].tick(at, "mid"))
                        dve.wait_ge(*free[3].after(at, "cos"))
                        dve.wait_ge(*free[0].after(at, "mid"))
                        for half in range(2):
                            s = slice(half * HALF, (half + 1) * HALF)
                            V.scalar_tensor_tensor(yf[:, s], yf[:, s], float(L) ** -0.5 * 0.5 / WS, zg[:, s], ALU.mult, ALU.mult)\
                                .then_inc(*o_in.tick(at, ("f", half)))

                    def per_head(t, d, c):
                        return t[:, d, c, :].unsqueeze(2).to_broadcast([P, HG, HD])

                    def masked(i):
                        if i:
                            dve.wait_ge(*w_ready.after(at, i - 1))
                        dve.wait_ge(*full[5].after(at, ("cb", i)))
                        V.tensor_tensor(cbm[:, 0, :], bank[5][:, 0:P], cst[:, LE, :], ALU.mult)
                        V.tensor_tensor(cbm[:, 1, :], bank[5][:, 0:P], cst[:, GE, :], ALU.mult)\
                            .then_inc(*free[5].tick(at, ("cb", i)))

                    def decayed(i):
                        dve.wait_ge(*w_ready.after(at, i))
                        dve.wait_ge(*free[6].after(at, ("seg", i)))
                        V.tensor_tensor(Mx[:], E[:], W[:, 0], ALU.mult).then_inc(*m_ready.tick(at, i))

                    masked(0)
                    decayed(0)
                    for i in range(PT):
                        if 3 <= i < 7:
                            j = i - 3
                            dve.wait_ge(*full[4].after(at, ("sc", j)))
                            link(V.tensor_reduce(att[:, 0, 0:2], bank[4][:].rearrange("p (n m) -> p n m", n=2), AX.X, ALU.max))
                            V.tensor_scalar(att[:, 0, 0:2], att[:, 0, 0:2], -float(P) ** -0.5, None, ALU.mult)\
                                .then_inc(*dve_s.tick(at, ("max", j)))
                        if i < PT - 1:
                            masked(i + 1)
                        if 3 <= i < 7:
                            dve.wait_ge(*free[4].after(at, ("sc", j)))
                            link(V.reciprocal(att[:, 2, 0:2], att[:, 1, 0:2]))
                            for n in range(2):
                                op = V.tensor_scalar(probs[:, j, n, :], probs[:, j, n, :], att[:, 2, n:n + 1], None, ALU.mult)
                            op.then_inc(*dve_s.tick(at, ("pr", j)))
                        if i == 1:
                            spectrum()
                        elif i == 2:
                            for half in range(2):
                                dve.wait_ge(*o_hi[half].after(at, ("f", half)))
                                V.tensor_tensor(st16[:, half, 1, :], yf[:, half * HALF:(half + 1) * HALF], st16[:, half, 0, :], ALU.subtract)\
                                    .then_inc(*o_lo[half].tick(at, ("f", half)))
                        if 2 <= i < 4:
                            gate(i, "QM", zg[:, (i - 2) * HALF:(i - 1) * HALF])
                        elif i >= 4:
                            gate(i - 4, "Z", zs[:, 2 * i - 8:2 * i - 6, :].rearrange("p t c -> p (t c)"))
                        if i == 5:
                            split_slab(0)
                        if i == 0:
                            dve.wait_ge(*pool_init.after(at, "Y"))
                        b = PT - 1 - i
                        yv = Y[:].rearrange("p t (h d) -> p t h d", h=HG)
                        dve.wait_ge(*full[4].after(at, ("bw", i)))
                        link(V.tensor_tensor(yt[:, 1], bank[4][:, 0:COLS].rearrange("p (h d) -> p h d", h=HG), per_head(gea, 1, b), ALU.mult))
                        V.tensor_tensor(yv[:, b], yv[:, b], yt[:, 1], ALU.add)
                        link(V.tensor_tensor(S[:, 1], S[:, 1], per_head(gtot, 1, b), ALU.mult))
                        V.tensor_tensor(S[:, 1], S[:, 1], bank[4][:, COLS:HALF].rearrange("p (h d) -> p h d", h=HG), ALU.add)\
                            .then_inc(*free[4].tick(at, ("bw", i)))
                        dve.wait_ge(*full[7].after(at, ("in", i)))
                        link(V.tensor_tensor(yt[:, 0], bank[7][:, COLS:HALF].rearrange("p (h d) -> p h d", h=HG), per_head(gea, 0, i), ALU.mult))
                        link(V.tensor_tensor(yt[:, 0], yt[:, 0], bank[7][:, 0:COLS].rearrange("p (h d) -> p h d", h=HG), ALU.add))
                        V.tensor_tensor(yv[:, i], yv[:, i], yt[:, 0], ALU.add).then_inc(*free[7].tick(at, ("in", i)))
                        dve.wait_ge(*full[5].after(at, ("st", i)))
                        link(V.tensor_tensor(S[:, 0], S[:, 0], per_head(gtot, 0, i), ALU.mult))
                        V.tensor_tensor(S[:, 0], S[:, 0], bank[5][:, 0:COLS].rearrange("p (h d) -> p h d", h=HG), ALU.add)\
                            .then_inc(*free[5].tick(at, ("st", i)))
                        dve.wait_ge(*free[5].after(at, ("st", i)))
                        if i < PT - 1:
                            dve.sem_inc(*s_ready[0].tick(at, i + 1))
                            dve.sem_inc(*s_ready[1].tick(at, i + 1))
                            decayed(i + 1)
                        if i == 2:
                            split_slab(1)
                    for q in range(4):
                        V.scalar_tensor_tensor(Y[:, 2 * q:2 * q + 2, :], Y[:, 2 * q:2 * q + 2, :], 0.5 / WS,
                                               zs[:, 2 * q:2 * q + 2, :], ALU.mult, ALU.mult).then_inc(*dve_s.tick(at, ("yg", q)))
                    inverse_rms(slice(0, PT), COLS)
                    settle(dve_s)
                    for t in range(PT):
                        op = V.scalar_tensor_tensor(Y[:, t, :], Y[:, t, :], rr[:, t:t + 1], ssdg[:, bass.ds(g * COLS, COLS)],
                                                    ALU.mult, ALU.mult)
                    op.then_inc(*dve_s.tick(at, "yn"))
                    split_slab(1)
                    for half in range(2):
                        dve.wait_ge(*full[6 + half].after(at, ("pv", half)))
                        V.scalar_tensor_tensor(qs[:], bank[6 + half][:], 0.5 / WS, zg[:, half * HALF:(half + 1) * HALF],
                                               ALU.mult, ALU.mult).then_inc(*free[6 + half].tick(at, ("pv", half)))
                        dve.wait_ge(*free[6 + half].after(at, ("pv", half)))
                        dve.sem_inc(*o_in.tick(at, ("m", half)))
                        dve.wait_ge(*o_hi[half].after(at, ("m", half)))
                        V.tensor_tensor(st16[:, half, 1, :], qs[:], st16[:, half, 0, :], ALU.subtract)\
                            .then_inc(*o_lo[half].tick(at, ("m", half)))
                        settle(o_lo[half])
                    split_slab(0)
                    for n in range(4):
                        r = (2, 3, 0, 1)[n]
                        dve.wait_ge(*o_hi[r].after(at, ("s", n)))
                        V.tensor_tensor(place[r][:, 1, :], bank[4 + n][:], place[r][:, 0, :], ALU.subtract)\
                            .then_inc(*free[4 + n].tick(at, ("ty", n)))
                        dve.wait_ge(*free[4 + n].after(at, ("ty", n)))
                        dve.sem_inc(*o_lo[r].tick(at, ("s", n)))

                at.enter("merge", lay)
                for j in range(4):
                    p0 = j % 2
                    if j:
                        split_slab(1 - p0)
                        split_slab(p0)
                    for q in range(4):
                        dve.wait_ge(*(free[q].after(at, (f"G0{j}", q)) if j else act_s.after(at, ("g0", q))))
                        dve.wait_ge(*full[q].after(at, (f"PS{j}", q)))
                        V.scalar_tensor_tensor(acc[:, q, :], tg[:, (3 * j) % 2, q, :], 1.0, bank[q][:], ALU.add, ALU.mult)\
                            .then_inc(*free[q].tick(at, (f"PS{j}", q)))
                        dve.wait_ge(*free[q].after(at, (f"PS{j}", q)))
                        dve.sem_inc(*t_used.tick(at, (0, j, q)))
                        if q == 0:
                            split_slab(1 - p0)
                    split_slab(p0)
                    for b, name in ((1, "PF"), (2, "PM")):
                        for q in range(4):
                            dve.wait_ge(*free[q].after(at, (f"G{b}{j}", q)))
                            dve.wait_ge(*full[q].after(at, (f"{name}{j}", q)))
                            part = tg[:, (3 * j + b) % 2, q, :]
                            V.scalar_tensor_tensor(part, part, 1.0, bank[q][:], ALU.add, ALU.mult)\
                                .then_inc(*free[q].tick(at, (f"{name}{j}", q)))
                            dve.wait_ge(*free[q].after(at, (f"{name}{j}", q)))
                            V.tensor_tensor(acc[:, q, :], acc[:, q, :], part, ALU.add).then_inc(*t_used.tick(at, (b, j, q)))
                            if b == 1 and q == 0:
                                split_slab(1 - p0)
                            if b == 2:
                                settle(t_used)
                                dve.sem_inc(*m_in.tick(at, (j, q)))
                    for q in range(4):
                        half = slice((q % 2) * HALF, (q % 2 + 1) * HALF)
                        kt = 2 * j + q // 2
                        dve.wait_ge(*m_hi.after(at, (j, q)))
                        V.scalar_tensor_tensor(mT[:, 1, kt, half], acc[:, q, :], 0.5 / WS,
                                               mT[:, 0, kt, half], ALU.mult, ALU.subtract)\
                            .then_inc(*m_lo.tick(at, (j, q)))
                at.enter("out", lay)
                dve.wait_ge(*x_back.reached(x_back.begin(at) + 1))
                for s, name in enumerate(OUT_SLABS):
                    for q in range(4):
                        dve.wait_ge(*full[q].after(at, (name, q)))
                        xv = X[:, 2 * q:2 * q + 2, s * COLS:(s + 1) * COLS]
                        V.scalar_tensor_tensor(xv, bank[q][:].rearrange("p (t c) -> p t c", t=2), 1 / WS, xv, ALU.mult, ALU.add)\
                            .then_inc(*free[q].tick(at, (name, q)))
                        if q == 0 and s < 3:
                            split_slab(1 - s % 2)
                        if s == 3 and q % 2 == 1:
                            dve.wait_ge(*free[q].after(at, (name, q)))
                            half_rms(q // 2)
                dve.wait_ge(*free[3].after(at, ("O3", 3)))
                dve.sem_inc(*x_done.tick(at, "X"))
            at.enter("post")
            dve.wait_ge(*dve_s.reached(dve_s.begin(at)))
            for t in range(4, PT):
                normalise(t)

        @block.gpsimd
        def _(pool):
            at = At()
            at.enter("pre")
            Q = nc.gpsimd

            def heads(t, *at_):
                return t.unsqueeze(2).to_broadcast([P, HG, HD])

            with pool.Fori(0, DEPTH) as lay:
                with pool.Fori(0, G) as g:
                    at.enter("group", lay, g)

                    def bands(i):
                        if i >= 2:
                            pool.wait_ge(*full[6].after(at, ("seg", i - 2)))
                        for d, mask in ((0, LE), (1, GE)):
                            for n in range(2):
                                op = Q.tensor_tensor(bnd[:, i % 2, d, n], mask16[:, mask - LE, :].unsqueeze(1).to_broadcast([P, HG, P]),
                                                     gda[:, n, d, i, :].unsqueeze(2).to_broadcast([P, HG, P]), ALU.mult)
                        op.then_inc(*bnd_ready.tick(at, i))

                    def weighted(i):
                        j = PT - 1 - i
                        if i >= 2:
                            pool.wait_ge(*full[7].after(at, ("in", i - 2)))
                        for d, c in ((0, i), (1, j)):
                            op = Q.tensor_tensor(xw[:, i % 2, d], xs_p[:, c, :].rearrange("p (h d) -> p h d", h=HG),
                                                 heads(gdd[:, d, c, :]), ALU.mult)
                        op.then_inc(*x_ready.tick(at, i))

                    def timed(i):
                        pool.wait_ge(*free[5].after(at, ("cb", i)))
                        if i:
                            pool.wait_ge(*m_ready.after(at, i - 1))
                        for d in range(2):
                            op = Q.tensor_tensor(W[:, d], cbm[:, d, :].unsqueeze(1).to_broadcast([P, HG, P]),
                                                 gdt[:, d, i, :].unsqueeze(2).to_broadcast([P, HG, P]), ALU.mult)
                        op.then_inc(*pool_chain.tick(at, i))
                        pool.wait_ge(*pool_chain.now(at))
                        Q.tensor_tensor(W[:, 0], W[:, 0], W[:, 1], ALU.add).then_inc(*w_ready.tick(at, i))

                    pool.wait_ge(*dve_s.after(at, "gc"))
                    bands(0)
                    bands(1)
                    pool.wait_ge(*free[5].after(at, ("tx", 1)))
                    for t in range(PT):
                        op = Q.tensor_tensor(Y[:, t, :].rearrange("p (h d) -> p h d", h=HG),
                                             xs_p[:, t, :].rearrange("p (h d) -> p h d", h=HG), heads(gdk[:]), ALU.mult)
                    op.then_inc(*pool_init.tick(at, "Y"))
                    weighted(0)
                    for i in range(PT):
                        timed(i)
                        if i + 1 < PT:
                            weighted(i + 1)
                        if i + 2 < PT:
                            bands(i + 2)

    for a, b in zip(full, free):
        assert len({sum(times * len(one.seen.get(phase, ())) for phase, times in PHASES) for one in (a, b)}) == 1, a.name
    return {one.name: one.seen for one in lines}


def _slab(w):
    return w.reshape(KT, P, COLS).transpose(1, 0, 2).reshape(P, KT * COLS)


def _lay_out(inputs):
    import numpy as np

    w_in, w_kv = inputs["w_in"], inputs["w_kv"]
    z, xbc, dt, u, zf, q, zm, gt = 0, 1024, 3072, 3104, 3616, 4128, 4640, 5152
    slabs = []
    for i in range(DEPTH):
        w, kv = w_in[i], w_kv[i]
        for g in range(G):
            one = slice(g * P, (g + 1) * P)
            part = lambda m, off: m[:, off:][:, one]
            pair = lambda a, b: np.concatenate([a, b], axis=1)
            slabs += [w[:, xbc + g * COLS:xbc + (g + 1) * COLS],
                      pair(part(w, xbc + 1024), part(w, xbc + 1536)),
                      pair(part(kv, 0), part(kv, 512)),
                      pair(part(w, u), part(w, zf)),
                      pair(part(w, q), part(w, zm)),
                      w[:, z + g * COLS:z + (g + 1) * COLS]]
        for j in range(4):
            c = slice(j * COLS, (j + 1) * COLS)
            gates = [w[:, gt + b * D:gt + (b + 1) * D][:, c] for b in range(3)]
            fm = np.concatenate([inputs["p_fno"][i][:, c], inputs["p_mem"][i][:, c]], axis=0)
            slabs += [gates[0], gates[1], inputs["p_ssd"][i][:, c], gates[2], fm]
        slabs += [inputs["w_out"][i][:, s * COLS:(s + 1) * COLS] for s in range(4)]
    wdt = np.stack([w_in[i][:, dt:dt + 32].reshape(KT, P, 32).transpose(1, 0, 2).reshape(P, KT * 32) for i in range(DEPTH)])
    par = []
    for i in range(DEPTH):
        cw = inputs["conv_w"][i].T.reshape(16, P, 5)
        cb = inputs["conv_b"][i].reshape(16, P)
        order = [b for g in range(G) for b in (2 * g, 2 * g + 1, 8 + g, 12 + g)]
        rows = np.concatenate([inputs["dt_bias"][i].reshape(-1), inputs["a_log"][i].reshape(-1), inputs["d_skip"][i]])
        par.append(np.concatenate([cw[order].transpose(1, 0, 2).reshape(P, 80), cb[order].T,
                                   np.broadcast_to(rows, (P, 80))], axis=1))
    return np.stack([_slab(s) for s in slabs]), wdt, np.stack(par)


def _tables():
    import numpy as np

    p, f = np.arange(P)[:, None], np.arange(P)[None, :]
    turn = 2 * np.pi * p * f / P
    cst = np.stack([np.cos(turn) * P ** -0.5, np.sin(turn) * P ** -0.5, p <= f, p >= f, p > f, p < f, p == f,
                    np.ones((P, P))], axis=1).astype(np.float32)
    l, k = np.arange(COLS)[:, None], np.arange(HALF)[None, :]
    turn = 2 * np.pi * (l * k % L) / L
    cos, sin = np.cos(turn), np.sin(turn)
    sin[0] = np.round(np.sin(np.pi / 2 * np.arange(HALF)))
    dft = np.zeros((P, 2, 2, 4, COLS), np.float16)
    for n, table in enumerate((cos, sin)):
        for odd in range(2):
            t = table[:, odd::2].reshape(2, P, COLS).transpose(1, 0, 2)
            hi = t.astype(np.float16)
            dft[:, n, 0, 2 * odd:2 * odd + 2], dft[:, n, 1, 2 * odd:2 * odd + 2] = hi, (t - hi).astype(np.float16)
    sign = (1 - 2 * (np.arange(COLS) % 2)).astype(np.float16)
    return cst, dft.reshape(P, -1), np.repeat(sign[:P, None], 2, axis=1), sign[None, :]


def kernel(**inputs):
    import numpy as np
    import concourse.bacc as bacc
    from concourse.bass_utils import run_bass_kernel_spmd

    inputs = {n: np.asarray(a) for n, a in inputs.items()}
    slabs, wdt, par = _lay_out(inputs)
    cst, dft, altc, altr = _tables()
    arrays = {"x": inputs["x"][0], "mem": inputs["mem"][0], "slabs": slabs, "wdt": wdt, "par": par,
              "gains": np.concatenate([inputs["norm_g"], inputs["final_g"][None]]), "mem_norm_g": inputs["mem_norm_g"], "ssd_norm_g": inputs["ssd_norm_g"],
              "cst": cst, "dft": dft, "altc": altc, "altr": altr}
    arrays = {f"in_{n}": np.ascontiguousarray(a) for n, a in arrays.items()}

    def program(plan):
        nc = bacc.Bacc("TRN2", target_bir_lowering=False, num_devices=1)
        io = [nc.dram_tensor(n, a.shape, mybir.dt.from_np(a.dtype), kind="ExternalInput").ap() for n, a in arrays.items()]
        io.append(nc.dram_tensor("out_0", (L, D), F32, kind="ExternalOutput").ap())
        io.append(nc.dram_tensor("x_scratch", (L, D), F32, kind="Internal").ap())
        io.append(nc.dram_tensor("y_scratch", (16, P, 2 * L), F16, kind="Internal").ap())
        return nc, build(nc, io, plan)

    _, plan = program(None)
    nc, _ = program(plan)
    r = run_bass_kernel_spmd(nc, [arrays], core_ids=[0])
    return r.results[0]["out_0"].reshape(1, L, D)
```
